# Optimizing a Trainium2 kernel written in Bass

```python
import math
import jax, jax.numpy as jnp
from jax import lax
import numpy as np

D_MODEL = 1024
BATCH = 1
SEQ = 256
DEPTH = 2

CHUNK = 64
N_A = DEPTH // 2
N_B = DEPTH - N_A
N_DENSE = (DEPTH + 1) // 2
N_MOE = DEPTH // 2

RET_HEADS = 8
RET_DK = D_MODEL // RET_HEADS
RET_DV = 2 * D_MODEL // RET_HEADS
RET_IN = 2 * RET_HEADS * RET_DK + 2 * RET_HEADS * RET_DV
ROPE_BASE = 10000.0

SB_HEADS = 16
SB_DH = D_MODEL // SB_HEADS
Q_BLOCK = 128

FF_DENSE = 2816
N_EXPERTS = 8
TOP_K = 2
FF_EXPERT = 3584
EPS = 1e-6

kernel_name = "yoco_retention_stickbreaking_moe_adaln"

def rms_norm(x, g):
    x32 = x.astype(jnp.float32)
    y = x32 * lax.rsqrt(jnp.mean(x32 * x32, axis=-1, keepdims=True) + EPS)
    return (y * g.astype(jnp.float32)).astype(x.dtype)

def modulate(h, shift, scale):
    return h * (1.0 + scale[:, None, :]) + shift[:, None, :]

def rope(t, cos, sin):
    t1, t2 = jnp.split(t, 2, axis=-1)
    return jnp.concatenate([t1 * cos - t2 * sin, t1 * sin + t2 * cos], axis=-1)

def retention(h, positions, w_in, gn_w, w_out):
    B, S, _ = h.shape
    H, DK, DV, C = RET_HEADS, RET_DK, RET_DV, CHUNK
    nC = S // C
    proj = h @ w_in
    q, k, v, g = jnp.split(proj, [H * DK, 2 * H * DK, 2 * H * DK + H * DV], axis=-1)
    q = q.reshape(B, S, H, DK)
    k = k.reshape(B, S, H, DK)
    v = v.reshape(B, S, H, DV)
    inv_freq = jnp.power(ROPE_BASE, -jnp.arange(0, DK, 2, dtype=jnp.float32) / DK)
    ang = positions.astype(jnp.float32)[..., None] * inv_freq
    cos = jnp.cos(ang)[:, :, None, :].astype(h.dtype)
    sin = jnp.sin(ang)[:, :, None, :].astype(h.dtype)
    q = rope(q, cos, sin)
    k = rope(k, cos, sin) * (DK ** -0.5)
    log_gamma = jnp.log(1.0 - jnp.exp2(-5.0 - jnp.arange(H, dtype=jnp.float32)))
    pos = jnp.arange(C, dtype=jnp.float32)
    d_intra = jnp.exp(jnp.abs(pos[:, None] - pos[None, :])[None] * log_gamma[:, None, None]).astype(h.dtype)
    q_decay = jnp.exp((pos[:, None] + 1.0) * log_gamma[None, :]).astype(h.dtype)
    k_decay = jnp.exp((C - 1.0 - pos)[:, None] * log_gamma[None, :]).astype(h.dtype)
    chunk_decay = jnp.exp(C * log_gamma).astype(h.dtype)

    def to_chunks(t):
        return jnp.moveaxis(t.reshape(B, nC, C, H, t.shape[-1]), 1, 0)

    def step(state, qkv):
        qc, kc, vc = qkv
        scores = jnp.einsum('bchd,bshd->bhcs', qc, kc) * d_intra[None]
        intra = jnp.einsum('bhcs,bshe->bche', scores, vc)
        cross = jnp.einsum('bchd,bhde->bche', qc * q_decay[None, :, :, None], state)
        new_state = state * chunk_decay[None, :, None, None] + jnp.einsum(
            'bshd,bshe->bhde', kc * k_decay[None, :, :, None], vc)
        return new_state, intra + cross

    state0 = jnp.zeros((B, H, DK, DV), dtype=q.dtype)
    _, o = lax.scan(step, state0, (to_chunks(q), to_chunks(k), to_chunks(v)))
    o = jnp.moveaxis(o, 0, 1).reshape(B, S, H, DV)
    o32 = o.astype(jnp.float32)
    mu = jnp.mean(o32, axis=-1, keepdims=True)
    var = jnp.mean(jnp.square(o32 - mu), axis=-1, keepdims=True)
    on = ((o32 - mu) * lax.rsqrt(var + EPS)).reshape(B, S, H * DV) * gn_w.astype(jnp.float32)
    return (jax.nn.silu(g) * on.astype(h.dtype)) @ w_out

def stick_breaking(h, k_sh, v_sh, w_q, w_out):
    B, S, _ = h.shape
    q = (h @ w_q).reshape(B, S, SB_HEADS, SB_DH)
    scale = SB_DH ** -0.5
    outs = []
    for i in range(S // Q_BLOCK):
        end = (i + 1) * Q_BLOCK
        qb = q[:, i * Q_BLOCK:end]
        kb = k_sh[:, :end]
        vb = v_sh[:, :end]
        z = jnp.einsum('bqhd,bkhd->bhqk', qb, kb).astype(jnp.float32) * scale
        t_idx = i * Q_BLOCK + jnp.arange(Q_BLOCK)
        s_idx = jnp.arange(end)
        causal = s_idx[None, :] < t_idx[:, None]
        log_one_minus = jnp.where(causal, jax.nn.log_sigmoid(-z), 0.0)
        tail = lax.cumsum(log_one_minus, axis=3, reverse=True) - log_one_minus
        a = jnp.where(causal, jnp.exp(jax.nn.log_sigmoid(z) + tail), 0.0)
        outs.append(jnp.einsum('bhqk,bkhd->bqhd', a.astype(vb.dtype), vb))
    o = jnp.concatenate(outs, axis=1).reshape(B, S, SB_HEADS * SB_DH)
    return o @ w_out

def swiglu(h, w_in, w_out):
    a, b = jnp.split(h @ w_in, 2, axis=-1)
    return (jax.nn.silu(a) * b) @ w_out

def moe_swiglu(h, router, w_in, w_out):
    B, S, D = h.shape
    hf = h.reshape(B * S, D)
    logits = (hf @ router).astype(jnp.float32)
    top_v, top_i = lax.top_k(logits, TOP_K)
    top_w = jax.nn.softmax(top_v, axis=-1)
    gates = jnp.sum(jax.nn.one_hot(top_i, N_EXPERTS, dtype=jnp.float32) * top_w[..., None], axis=1)
    y = jnp.zeros_like(hf)
    for e in range(N_EXPERTS):
        y = y + gates[:, e:e + 1].astype(hf.dtype) * swiglu(hf, w_in[e], w_out[e])
    return y.reshape(B, S, D)

def setup_inputs(seed: int = 0) -> dict:
    key = jax.random.key(seed)
    ks = jax.random.split(key, 24)
    D = D_MODEL

    def nrm(k, shape, fan_in, s=1.0):
        return jax.random.normal(k, shape, jnp.float32) * (s * fan_in ** -0.5)

    def gain(k, shape):
        return 1.0 + 0.02 * jax.random.normal(k, shape, jnp.float32)

    x = jax.random.normal(ks[0], (BATCH, SEQ, D), jnp.float32)
    c = jax.random.normal(ks[1], (BATCH, D), jnp.float32)
    offset = jax.random.randint(ks[2], (BATCH, 1), 0, 4096, dtype=jnp.int32)
    positions = offset + jnp.arange(SEQ, dtype=jnp.int32)[None, :]
    return {
        "x": x,
        "c": c,
        "positions": positions,
        "ada_w": nrm(ks[3], (DEPTH, D, 6 * D), D, 0.5),
        "ada_b": 0.02 * jax.random.normal(ks[4], (DEPTH, 6 * D), jnp.float32),
        "norm_mix": gain(ks[5], (DEPTH, D)),
        "norm_ff": gain(ks[6], (DEPTH, D)),
        "ret_w_in": nrm(ks[7], (N_A, D, RET_IN), D),
        "ret_gn": gain(ks[8], (N_A, RET_HEADS * RET_DV)),
        "ret_w_out": nrm(ks[9], (N_A, RET_HEADS * RET_DV, D), RET_HEADS * RET_DV),
        "kv_ada_w": nrm(ks[10], (D, 2 * D), D, 0.5),
        "kv_ada_b": 0.02 * jax.random.normal(ks[11], (2 * D,), jnp.float32),
        "kv_norm": gain(ks[12], (D,)),
        "kv_w": nrm(ks[13], (D, 2 * SB_HEADS * SB_DH), D),
        "sb_w_q": nrm(ks[14], (N_B, D, SB_HEADS * SB_DH), D),
        "sb_w_out": nrm(ks[15], (N_B, SB_HEADS * SB_DH, D), SB_HEADS * SB_DH),
        "ff_w_in": nrm(ks[16], (N_DENSE, D, 2 * FF_DENSE), D),
        "ff_w_out": nrm(ks[17], (N_DENSE, FF_DENSE, D), FF_DENSE),
        "moe_router": nrm(ks[18], (N_MOE, D, N_EXPERTS), D),
        "moe_w_in": nrm(ks[19], (N_MOE, N_EXPERTS, D, 2 * FF_EXPERT), D),
        "moe_w_out": nrm(ks[20], (N_MOE, N_EXPERTS, FF_EXPERT, D), FF_EXPERT),
        "final_norm": gain(ks[21], (D,)),
    }

def reference(x, c, positions, ada_w, ada_b, norm_mix, norm_ff, ret_w_in, ret_gn, ret_w_out,
              kv_ada_w, kv_ada_b, kv_norm, kv_w, sb_w_q, sb_w_out, ff_w_in, ff_w_out,
              moe_router, moe_w_in, moe_w_out, final_norm):
    B, S, _ = x.shape
    cond = jax.nn.silu(c)
    k_sh = None
    v_sh = None
    for i in range(DEPTH):
        mod = cond @ ada_w[i] + ada_b[i]
        sh_m, sc_m, g_m, sh_f, sc_f, g_f = jnp.split(mod, 6, axis=-1)
        h = modulate(rms_norm(x, norm_mix[i]), sh_m, sc_m)
        if i < N_A:
            y = retention(h, positions, ret_w_in[i], ret_gn[i], ret_w_out[i])
        else:
            j = i - N_A
            y = stick_breaking(h, k_sh, v_sh, sb_w_q[j], sb_w_out[j])
        x = x + g_m[:, None, :] * y
        h = modulate(rms_norm(x, norm_ff[i]), sh_f, sc_f)
        if i % 2 == 0:
            y = swiglu(h, ff_w_in[i // 2], ff_w_out[i // 2])
        else:
            y = moe_swiglu(h, moe_router[i // 2], moe_w_in[i // 2], moe_w_out[i // 2])
        x = x + g_f[:, None, :] * y
        if i == N_A - 1:
            kv_mod = cond @ kv_ada_w + kv_ada_b
            sh_kv, sc_kv = jnp.split(kv_mod, 2, axis=-1)
            hk = modulate(rms_norm(x, kv_norm), sh_kv, sc_kv)
            kv = (hk @ kv_w).reshape(B, S, 2, SB_HEADS, SB_DH)
            k_sh = kv[:, :, 0]
            v_sh = kv[:, :, 1]
    return rms_norm(x, final_norm)


_drawn_inputs = setup_inputs


def setup_inputs(seed=0):
    import zlib

    import numpy as np

    out = dict(_drawn_inputs(seed))
    spreads = {}
    factors = {'norm_mix': 5.543,
     'norm_ff': 4.844,
     'ret_gn': 8.0,
     'kv_ada_b': 6.269,
     'kv_norm': 25.569,
     'final_norm': 7.467}
    for name, (base, spread) in spreads.items():
        noise = np.random.default_rng([zlib.crc32(name.encode()), seed]).standard_normal(out[name].shape)
        drawn = base * np.exp(spread * noise) if base else spread * noise
        out[name] = __import__('jax').numpy.asarray(drawn.astype(out[name].dtype))
    for name, factor in factors.items():
        out[name] = (out[name] * factor).astype(out[name].dtype)
    return out
```

```python
from contextlib import ExitStack

import numpy as np
import concourse.bass as bass
from concourse import mybir

P = 128
S = 256
D = 1024
NB = S // P
KC = D // P
TW = 512
RET_HEADS, DK, DV, CHUNK = 8, 128, 256, 64
PAIRS = RET_HEADS // 2
SB_HEADS, DH = 16, 64
FF = 2816
FW = 256
FT = FF // FW
NE, FE = 8, 3584
ET = FE // TW
EPS = 1e-6
RAW, RING = 6, 3
DMA_SCRATCH = 2048
PAIR_STEPS = 16
HALF = 2048

U_RET = 0
U_OUT = U_RET + 6 * PAIRS
U_FF = U_OUT + 8
U_KV = U_FF + 3 * FT
U_Q = U_KV + 8
U_SBO = U_Q + 4
U_MOE = U_SBO + 4
MOE_U = 6 * ET

SH, SC, G = 0, 8, 16
MIX0, FF0, KVM, MIX1, FF1 = 0, 24, 48, 64, 88
V_MIX, V_FF, V_KVN, V_GN, V_C = 112, 128, 144, 152, 168


def trunk(nc, x_d, c_d, pos_d, ada_w, ada_b, norm_mix, norm_ff, ret_w_in, ret_gn, ret_w_out, kv_ada_w,
          kv_ada_b, kv_norm, kv_w, sb_w_q, sb_w_out, ff_w_in, ff_w_out, router, moe_w_in, moe_w_out,
          final_norm, decay_d, freq_d, out_d):
    f32, f32r, i32, u32 = mybir.dt.float32, mybir.dt.float32r, mybir.dt.int32, mybir.dt.uint32
    ALU, ACT, AX = mybir.AluOpType, mybir.ActivationFunctionType, mybir.AxisListType
    ds = bass.ds

    ctx = ExitStack()
    with ctx:
        def sb(name, shape, dt=f32):
            return ctx.enter_context(nc.sbuf_tensor(name, shape, dt))

        def sem(name):
            return ctx.enter_context(nc.semaphore(name))

        raw = sb("raw", [P, RAW, HALF])
        w_hi = sb("w_hi", [P, RING, HALF], f32r)
        w_lo = sb("w_lo", [P, RING, HALF], f32r)
        x = sb("x", [P, NB, D])
        hT_hi = sb("hT_hi", [P, KC, S], f32r)
        hT_lo = sb("hT_lo", [P, KC, S], f32r)
        ada = sb("ada", [P, 2, HALF])
        acc = sb("acc", [P, 2, TW])
        gate_m = sb("gate_m", [P, D])
        gate_f = sb("gate_f", [P, D])
        RA = sb("RA", [P, 8192], f32r)
        FA = sb("FA", [P, 9216])
        ident = sb("ident", [P, P])
        ones = sb("ones", [P, P])
        before = sb("before", [P, P])
        after = sb("after", [P, P])
        slot_no = sb("slot_no", [P, P])
        causal = sb("causal", [P, 384])
        vec = sb("vec", [P, 176])
        modc = sb("modc", [P, 112])
        cond = sb("cond", [P, KC])
        scol = sb("scol", [P, 5, KC])
        cos, sin = (gate_m[:, n * P:(n + 1) * P].rearrange("p (b f) -> p b f", b=NB) for n in range(2))
        stat = sb("stat", [P, 64])
        mv = sb("mv", [P, 4, 2])
        ridx = sb("ridx", [P, NB, 8], u32)
        npass_t = sb("npass_t", [P, 1], i32)
        pos_i = sb("pos_i", [P, NB], i32)
        ps = ctx.enter_context(nc.psum_tensor("ps", [P, 8, 512], f32))

        def fa(off, *shape):
            n = int(np.prod(shape))
            v = FA[:, off:off + n]
            if len(shape) == 1:
                return v
            names = "abcd"[:len(shape)]
            return v.rearrange(f"p ({' '.join(names)}) -> p {' '.join(names)}", **dict(zip(names, shape)))

        def ra(off, *shape):
            n = int(np.prod(shape))
            v = RA[:, off:off + n]
            if len(shape) == 1:
                return v
            names = "abcd"[:len(shape)]
            return v.rearrange(f"p ({' '.join(names)}) -> p {' '.join(names)}", **dict(zip(names, shape)))

        qk = fa(0, NB, 512)
        qkr = fa(1024, NB, 512)
        v_t = fa(2048, NB, 512)
        gs = fa(3072, NB, 512)
        r32 = fa(4096, 4, S)
        qkT = fa(5120, 4, S)
        PT = fa(6144, 2, 384)
        decay = fa(6912, 2, 384)
        rope_t = fa(7680, 2, 512)
        rT_hi = ra(0, 16, S)
        rT_lo = ra(4096, 16, S)
        diag0, diag1 = fa(1024, KC, P), fa(0, KC, P)
        xn = fa(6144, NB, D)
        xn0 = fa(2048, NB, D)
        h32 = fa(6144, KC, S)
        h32_0 = fa(2048, KC, S)

        def h32_at(q):
            return h32_0 if q == 0 else h32

        f_sa = fa(0, NB, FW)
        f_g = fa(512, NB, FW)
        f_tmp = fa(1024, NB, D)
        fT_hi = ra(0, 2, S)
        fT_lo = ra(512, 2, S)
        v_all = fa(0, NB, D)
        qT = fa(2048, KC, S)
        kT = fa(4096, KC, S)
        qk_t = fa(8192, NB, 512)
        diag2 = fa(8192, KC, P)
        oT_hi = ra(0, KC, S)
        oT_lo = ra(2048, KC, S)
        ada_flat = ada[:, :, :].rearrange("p a b -> p (a b)")
        diag3 = ada_flat[:, 3072:4096].rearrange("p (c q) -> p c q", c=KC)

        def at_buf(c, n):
            src = FA[:, 6144:9216] if c % 2 == 0 else ada_flat[:, 0:3072]
            return src[:, n * 768:(n + 1) * 768].rearrange("p (h t) -> p h t", h=2)

        y_acc = fa(0, NB, D)
        e_sa = fa(2048, TW)
        e_g = fa(2560, TW)
        hk_hi = hT_hi[:, :, :].rearrange("p c s -> p (c s)").rearrange("p (b d) -> p b d", b=NB)
        hk_lo = hT_lo[:, :, :].rearrange("p c s -> p (c s)").rearrange("p (b d) -> p b d", b=NB)
        hg_hi = ra(0, KC, P)
        hg_lo = ra(1024, KC, P)
        eT_hi = ra(2048, 4, P)
        eT_lo = ra(2560, 4, P)
        hot = ra(3072, NB, P)
        hotT = ra(3328, S)
        y_hi = ra(3584, D)
        y_lo = ra(4608, D)
        logit, gate_e, sel, slot, oh1, oh2, mx = (fa(3072 + 16 * n, NB, NE) for n in range(7))
        rw = fa(3328, KC, NE)
        rw_hi = ra(4096, KC, NE)
        rw_lo = ra(4160, KC, NE)
        freq = FA[:, 0:64]
        ang, red, kk, tmp_r = (fa(64 + 128 * n, NB, 64) for n in range(4))
        k_int = fa(64 + 128 * 4, NB, 64).bitcast(i32)
        rows = fa(1024, 2, P)
        fnorm = fa(4096, D)

        small_in = sem("small_in"); pos_in = sem("pos_in"); x_in = sem("x_in"); rw_in = sem("rw_in")
        fnorm_in = sem("fnorm_in"); ang_ok = sem("ang_ok"); sd_n = sem("sd_n")
        rwh_ok = sem("rwh_ok"); const_ok = sem("const_ok"); pchain = sem("pchain")
        vecT_done = sem("vecT_done"); vec_ok = sem("vec_ok"); cond_ok = sem("cond_ok")
        w_in = [sem(f"w_in{n}") for n in range(RAW)]
        hi_done = sem("hi_done"); lo_done = sem("lo_done"); w_used = sem("w_used")
        ada_in = [sem("ada_in0"), sem("ada_in1")]
        ada_used = sem("ada_used"); acc_red = sem("acc_red"); mod_ok = sem("mod_ok")
        vchain = sem("vchain"); achain = sem("achain")
        decay_in = sem("decay_in")
        ss_ok = sem("ss_ok"); ms_ok = sem("ms_ok"); rt_ok = sem("rt_ok"); xn_ok = sem("xn_ok")
        xT_done = sem("xT_done"); h32_ok = sem("h32_ok"); h_hi_ok = sem("h_hi_ok"); h_ok = sem("h_ok")
        scol_ok = sem("scol_ok")
        qk_ev = sem("qk_ev"); v_ev = sem("v_ev"); gs_ok = sem("gs_ok"); roped = sem("roped")
        qkT_done = sem("qkT_done"); qkT_ev = sem("qkT_ev"); sc_done = sem("sc_done"); pt_ok = sem("pt_ok")
        pv_done = sem("pv_done"); var_ok = sem("var_ok"); sd_ok = sem("sd_ok"); r_ok = sem("r_ok")
        outT_done = sem("outT_done"); r32_ok = sem("r32_ok"); rTh_ok = sem("rTh_ok"); rTl_ok = sem("rTl_ok")
        diag_ok = sem("diag_ok"); gbc_done = sem("gbc_done"); gbc_ev = sem("gbc_ev")
        x_ok = sem("x_ok")
        fsa_ok = sem("fsa_ok"); fg_ok = sem("fg_ok"); fT_done = sem("fT_done")
        fTh_ok = sem("fTh_ok"); fTl_ok = sem("fTl_ok")
        kv_ev = sem("kv_ev"); kqT_done = sem("kqT_done"); kqT_ev = sem("kqT_ev")
        z_done = sem("z_done"); sm_ok = sem("sm_ok"); lm_ok = sem("lm_ok")
        tail_done = sem("tail_done"); u_ok = sem("u_ok"); a0_ok = sem("a0_ok"); am_ok = sem("am_ok")
        av_done = sem("av_done"); oh_ok = sem("oh_ok"); ol_ok = sem("ol_ok")
        rws_ok = sem("rws_ok"); rt_done = sem("rt_done"); dm_ok = sem("dm_ok"); ex_ok = sem("ex_ok")
        sel_ok = sem("sel_ok"); cnt_done = sem("cnt_done"); npass_ok = sem("npass_ok")
        hk_done = sem("hk_done"); hk_hi_ok = sem("hk_hi_ok"); hk_ok = sem("hk_ok"); yz_ok = sem("yz_ok")
        hot_ok = sem("hot_ok"); ga_done = sem("ga_done"); hgh_ok = sem("hgh_ok"); hgl_ok = sem("hgl_ok")
        hotT_done = sem("hotT_done"); hotT_ok = sem("hotT_ok")
        esa_ok = sem("esa_ok"); eg_ok = sem("eg_ok"); eT_done = sem("eT_done")
        eTh_ok = sem("eTh_ok"); eTl_ok = sem("eTl_ok"); yh_ok = sem("yh_ok")
        yl_ok = sem("yl_ok"); scat_done = sem("scat_done")
        o_ok = sem("o_ok"); stored = sem("stored")

        block = ctx.enter_context(nc.Block())

        def at(c, m=0):
            return c + RAW * m

        @block.sync
        def _(sp):
            def free(c, m=0):
                if c >= RAW:
                    sp.wait_ge(lo_done, at(c - RAW + 1, m))

            def cols_of(w, row, col, n):
                return w[ds(row, 4 * P), ds(col, n)].rearrange("(t p) n -> p t n", p=P)

            def slot4(c, lo, n):
                return raw[:, c % RAW, :].rearrange("p (t n) -> p t n", t=4)[:, :, lo:lo + n]

            def load_tile(c, m, w, row, col):
                for h in range(2):
                    load_half(c + h, m, w, row + h * 4 * P, col)

            def load_half(c, m, w, row, col):
                free(c, m)
                sp.dma_start(slot4(c, 0, TW), cols_of(w, row, col, TW)).then_inc(w_in[c % RAW], 32)

            def load_half2(c, m, w, row, col_a, col_b):
                free(c, m)
                for n, col in enumerate((col_a, col_b)):
                    sp.dma_start(slot4(c, n * FW, FW), cols_of(w, row, col, FW)).then_inc(w_in[c % RAW], 16)

            def load_rows(c, m, w, row):
                free(c, m)
                sp.dma_start(raw[:, c % RAW, :].rearrange("p (t n) -> p t n", t=2),
                             w[ds(row, 2 * P), :].rearrange("(t p) n -> p t n", p=P)).then_inc(w_in[c % RAW], 32)

            def load_ada(t, k, w, col):
                for h in range(2):
                    if t > 0:
                        sp.wait_ge(ada_used, 2 * t + h - 1 + 4 * k)
                    sp.dma_start(ada[:, h, :].rearrange("p (t n) -> p t n", t=4),
                                 cols_of(w, h * 4 * P, col, TW)).then_inc(ada_in[h], 16)

            for row, src in ((0, ada_b[0]), (48, kv_ada_b), (64, ada_b[1])):
                n = src.shape[0] // P
                sp.dma_start(rows[row:row + n, 0, :], src.rearrange("(r c) -> r c", c=P)).then_inc(small_in, 16)
            for row, g, src in ((112, 0, norm_mix.rearrange("l (r c) -> (l r) c", c=P)),
                                (0, 1, norm_ff.rearrange("l (r c) -> (l r) c", c=P)),
                                (16, 1, kv_norm.rearrange("(r c) -> r c", c=P)),
                                (24, 1, ret_gn[0].rearrange("(r c) -> r c", c=P)),
                                (40, 1, c_d[0].rearrange("(r c) -> r c", c=P))):
                sp.dma_start(rows[row:row + src.shape[0], g, :], src).then_inc(small_in, 16)
            load_ada(0, 0, ada_w[0], 0)
            sp.dma_start(x[:, :, :], x_d[0].rearrange("(b p) d -> p b d", p=P)).then_inc(x_in, 16)
            with nc.allow_non_contiguous_dma(reason="256 positions, one per partition"):
                sp.dma_start(pos_i[:, :], pos_d[0].rearrange("(b p) -> p b", p=P)).then_inc(pos_in, 16)
            sp.dma_start(freq, freq_d.to_broadcast([P, DK // 2])).then_inc(pos_in, 16)

            w_r = ret_w_in[0]
            K0, V0, G0 = RET_HEADS * DK, 2 * RET_HEADS * DK, 2 * RET_HEADS * DK + RET_HEADS * DV

            def load_qk(c, m, i):
                for h in range(2):
                    load_half2(c + h, m, w_r, h * 4 * P, i * 2 * DK, i * 2 * DK + K0)

            def load_decay(i):
                sp.dma_start(decay, decay_d[ds(i * P, P), :].rearrange("p (h t) -> p h t", h=2)).then_inc(decay_in, 16)

            load_qk(0, 0, 0)
            load_ada(1, 0, ada_w[0], TW)
            load_tile(2, 0, w_r, 0, V0)
            load_ada(2, 0, ada_w[0], 2 * TW)
            load_tile(4, 0, w_r, 0, G0)
            load_ada(3, 0, ada_w[0], 3 * TW)
            load_decay(0)
            load_ada(4, 0, ada_w[0], 4 * TW)
            with sp.Fori(0, PAIRS - 1) as k:
                load_qk(6, k, k + 1)
                load_tile(8, k, w_r, 0, k * 2 * DV + (V0 + 2 * DV))
                load_ada(5, k, ada_w[0], k * 2 * TW + 5 * TW)
                load_tile(10, k, w_r, 0, k * 2 * DV + (G0 + 2 * DV))
                load_ada(6, k, ada_w[0], k * 2 * TW + 6 * TW)
                sp.wait_ge(pt_ok, k + 1)
                load_decay(k + 1)

            for m in range(8):
                load_rows(U_OUT + m, 0, ret_w_out[0], m * 2 * P)
                if m == 3:
                    load_ada(11, 0, ada_w[0], 11 * TW)
                if m == 5:
                    load_ada(12, 0, kv_ada_w, 0)

            def load_in(c, m, j, h):
                load_half2(c, m, ff_w_in[0], h * 4 * P, j * FW, j * FW + FF)

            c = U_FF
            load_in(c, 0, 0, 0)
            load_in(c + 1, 0, 0, 1)
            load_ada(13, 0, kv_ada_w, TW)
            load_in(c + 2, 0, 1, 0)
            load_in(c + 3, 0, 1, 1)
            load_ada(14, 0, kv_ada_w, 2 * TW)
            load_rows(c + 4, 0, ff_w_out[0], 0)
            load_ada(15, 0, kv_ada_w, 3 * TW)
            load_in(c + 5, 0, 2, 0)
            load_ada(16, 0, ada_w[1], 0)
            load_in(c + 6, 0, 2, 1)
            load_rows(c + 7, 0, ff_w_out[0], 2 * P)
            load_in(c + 8, 0, 3, 0)
            load_in(c + 9, 0, 3, 1)
            load_rows(c + 10, 0, ff_w_out[0], 4 * P)
            with sp.Fori(0, 3) as k:
                for o in range(2):
                    for h in range(2):
                        load_in(c + 11 + 3 * o + h, k, 2 * k + (4 + o), h)
                    load_ada(17 + o, k, ada_w[1], k * 2 * TW + (1 + o) * TW)
                    load_rows(c + 13 + 3 * o, k, ff_w_out[0], k * 4 * P + (3 + o) * 2 * P)
            load_in(c + 29, 0, 10, 0)
            load_in(c + 30, 0, 10, 1)
            load_ada(23, 0, ada_w[1], 7 * TW)
            load_rows(c + 31, 0, ff_w_out[0], 9 * 2 * P)
            load_rows(c + 32, 0, ff_w_out[0], 10 * 2 * P)
            for n, col in enumerate((D, D + TW, 0, TW)):
                for h in range(2):
                    u = U_KV + 2 * n + h
                    load_half(u, 0, kv_w, h * 4 * P, col)
                    if u - U_KV in (0, 3):
                        t = 24 + (u - U_KV) // 3
                        load_ada(t, 0, ada_w[1], (t - 16) * TW)
                    if u - U_KV == 6:
                        load_ada(26, 0, ada_w[1], 10 * TW)
                        load_ada(27, 0, ada_w[1], 11 * TW)
            for t in range(2):
                load_tile(U_Q + 2 * t, 0, sb_w_q[0], 0, t * TW)
            for t in range(2):
                load_tile(U_SBO + 2 * t, 0, sb_w_out[0], 0, t * TW)

            w_ab = moe_w_in[0].rearrange("e k n -> (e k) n")
            w_dn = moe_w_out[0].rearrange("e k n -> (e k) n")

            def experts(m_pass):
                with sp.Fori(0, NE) as e:
                    me = ET * e + m_pass
                    for ab in range(2):
                        load_tile(U_MOE + 2 * ab, me, w_ab, e * D, ab * FE)
                    with sp.Fori(0, ET - 1) as k:
                        for ab in range(2):
                            load_tile(U_MOE + 4 + 2 * ab, me + k, w_ab, e * D, k * TW + (TW + ab * FE))
                        for h in range(2):
                            load_rows(U_MOE + 8 + h, me + k, w_dn, e * FE + k * TW + h * 2 * P)
                    for h in range(2):
                        load_rows(U_MOE + MOE_U - 2 + h, me, w_dn, e * FE + ((ET - 1) * TW + h * 2 * P))

            experts(0)
            sp.wait_ge(npass_ok, 1)
            npass = sp.value_load(npass_t[0:1, 0:1], min_val=1, max_val=2)
            with sp.If(npass - 1):
                experts(NE * ET)
            sp.wait_ge(z_done, KC)
            sp.dma_start(fnorm, final_norm.rearrange("(a d) -> a d", a=1).to_broadcast([P, D])).then_inc(fnorm_in, 16)
            sp.wait_ge(o_ok, 2)
            sp.dma_start(out_d[0].rearrange("(b p) d -> p b d", p=P), x[:, :, :]).then_inc(stored, 16)
            sp.wait_ge(stored, 16)

        @block.gpsimd
        def _(pool):
            steps = Chain(pool, pchain)
            steps.link(pool.memset(ones[:, :], 1.0))
            pool.memset(causal[:, :], 1.0)
            steps.link(pool.iota(slot_no[:, :], pattern=[[1, P]], base=0, channel_multiplier=0,
                                 allow_small_or_imprecise_dtypes=True))
            pool.affine_select(out=ident[:, :], in_=ones[:, :], compare_op=ALU.is_equal, fill=0.0, base=0,
                               pattern=[[-1, P]], channel_multiplier=1)
            pool.affine_select(out=before[:, :], in_=ones[:, :], compare_op=ALU.is_gt, fill=0.0, base=0,
                               pattern=[[1, P]], channel_multiplier=-1)
            pool.affine_select(out=after[:, :], in_=ones[:, :], compare_op=ALU.is_gt, fill=0.0, base=0,
                               pattern=[[-1, P]], channel_multiplier=1)
            pool.affine_select(out=causal[:, 0:S], in_=causal[:, 0:S], compare_op=ALU.is_gt, fill=0.0, base=0,
                               pattern=[[1, S]], channel_multiplier=-1)
            pool.affine_select(out=causal[:, S:384], in_=causal[:, S:384], compare_op=ALU.is_gt, fill=0.0, base=0,
                               pattern=[[1, P]], channel_multiplier=-1).then_inc(const_ok, 1)

            def rope(i, per=5):
                cs, sn = (t[:, :, :].unsqueeze(2).to_broadcast([P, NB, 4, DK // 2]) for t in (cos, sin))
                src = qk.rearrange("p b (g r f) -> p b g r f", g=4, r=2)
                dst = qkr.rearrange("p b (g r f) -> p b g r f", g=4, r=2)
                t1, t2, o1, o2 = src[:, :, :, 0, :], src[:, :, :, 1, :], dst[:, :, :, 0, :], dst[:, :, :, 1, :]
                ta, tb = (rope_t[:, n, :].rearrange("p (b g f) -> p b g f", b=NB, g=4) for n in range(2))
                pool.wait_ge(qk_ev, i + 1)
                pool.tensor_tensor(ta, t1, cs, ALU.mult)
                steps.link(pool.tensor_tensor(tb, t2, sn, ALU.mult))
                if not isinstance(i, int):
                    pool.wait_ge(qkT_done, i)
                steps.link(pool.tensor_tensor(o1, ta, tb, ALU.subtract))
                pool.tensor_tensor(ta, t1, sn, ALU.mult)
                steps.link(pool.tensor_tensor(tb, t2, cs, ALU.mult))
                pool.tensor_tensor(o2, ta, tb, ALU.add).then_inc(roped, 1)

            pool.wait_ge(rt_ok, 2)
            rope(0)
            with pool.Fori(0, PAIRS - 1) as k:
                steps.enter(k, 3)
                rope(k + 1)
                steps.leave(PAIRS - 1)

            mask = causal[:, :].unsqueeze(1).to_broadcast([P, 2, 384])
            for c in range(KC):
                pool.wait_ge(a0_ok, c + 1)
                pool.tensor_tensor(at_buf(c, 3), at_buf(c, 3), mask, ALU.mult).then_inc(am_ok, 1)

            pool.wait_ge(x_ok, 3)
            pool.memset(y_acc, 0.0).then_inc(yz_ok, 1)

        @block.tensor
        def _(pe):
            def passes(out, a_hi, a_lo, b_hi, b_lo, first, last):
                pe.matmul(out, a_hi, b_hi, start=first, stop=False)
                pe.matmul(out, a_hi, b_lo, start=False, stop=False)
                return pe.matmul(out, a_lo, b_hi, start=False, stop=last)

            def landed(c, m=0):
                pe.wait_ge(lo_done, at(c + 1, m))

            def by_rows(c, m, a_hi, a_lo, kc0, blocks, bank0, first, last_one):
                landed(c, m)
                s = c % RING
                for t in range(2):
                    for b in range(blocks):
                        tok = slice(b * P, (b + 1) * P)
                        for n in range(2):
                            cols = slice(t * D + n * TW, t * D + (n + 1) * TW)
                            last = passes(ps[:, bank0 + 2 * b + n, :], a_hi[:, kc0 + t, tok], a_lo[:, kc0 + t, tok],
                                          w_hi[:, s, cols], w_lo[:, s, cols], first and t == 0, last_one and t == 1)
                last.then_inc(w_used, 1)

            def reduce_ada(pair, k, bank):
                pe.wait_ge(ada_used, 4 * (pair + 1) + 4 * k)
                for t in range(2):
                    for c in range(4):
                        last = pe.matmul(ps[:, bank, 4 * t + c:4 * t + c + 1], acc[:, t, c * P:(c + 1) * P],
                                         ones[:, 0:1], start=True, stop=True)
                last.then_inc(acc_red, 1)

            def transpose_x(n):
                for b in range(NB):
                    pe.wait_ge(xn_ok, 2 * n + b + 1)
                    for c in range(KC):
                        last = pe.transpose(ps[:, c // 2, (c % 2) * S + b * P:(c % 2) * S + (b + 1) * P],
                                            (xn0 if n == 0 else xn)[:, b, c * P:(c + 1) * P], ident[:, :])
                last.then_inc(xT_done, 1)

            def broadcast_gate(g, dg, bank):
                pe.wait_ge(diag_ok, g + 1)
                for n in range(2):
                    last = pe.matmul(ps[:, bank + n, :], ones[:, :],
                                     dg[:, 4 * n:4 * n + 4, :].rearrange("p c q -> p (c q)"), start=True, stop=True)
                last.then_inc(gbc_done, 1)

            pe.wait_ge(const_ok, 1)
            pe.wait_ge(small_in, 8 * 16)
            pe.transpose(ps[:, 4, 0:P], rows[:, 0, :], ident[:, :])
            pe.transpose(ps[:, 4, P:P + 48], rows[0:48, 1, :], ident[0:48, 0:48]).then_inc(vecT_done, 1)
            transpose_x(0)
            reduce_ada(0, 0, 4)
            pe.wait_ge(mod_ok, 1)
            reduce_ada(1, 0, 4)

            def transpose_r(i):
                pe.wait_ge(r_ok, i + 1)
                for c in range(4):
                    for b in range(NB):
                        last = pe.transpose(ps[:, 6 + c // 2, (c % 2) * S + b * P:(c % 2) * S + (b + 1) * P],
                                            gs[:, b, c * P:(c + 1) * P], ident[:, :])
                last.then_inc(outT_done, 1)

            def tile(c, m, banks):
                for h in range(2):
                    landed(c + h, m)
                    s = (c + h) % RING
                    for t in range(4):
                        kc = 4 * h + t
                        cols = slice(t * TW, (t + 1) * TW)
                        for b, bank in enumerate(banks):
                            tok = slice(b * P, (b + 1) * P)
                            last = passes(ps[:, bank, :], hT_hi[:, kc, tok], hT_lo[:, kc, tok],
                                          w_hi[:, s, cols], w_lo[:, s, cols], kc == 0, kc == KC - 1)
                    last.then_inc(w_used, 1)

            def pair_of_heads(i, m):
                later = not isinstance(i, int)
                if later:
                    pe.wait_ge(gs_ok, i)
                tile(0, m, (0, 1))
                if later:
                    pe.wait_ge(pt_ok, i)
                    transpose_r(i - 1)
                    pe.wait_ge(v_ev, i)
                tile(2, m, (2, 3))
                pe.wait_ge(roped, i + 1)
                if not later:
                    pe.wait_ge(mod_ok, 2)
                for g in range(4):
                    for b in range(NB):
                        last = pe.transpose(ps[:, 4 + g // 2, (g % 2) * S + b * P:(g % 2) * S + (b + 1) * P],
                                            qkr[:, b, g * P:(g + 1) * P], ident[:, :])
                last.then_inc(qkT_done, 1)
                pe.wait_ge(qk_ev, i + 1)
                tile(4, m, (0, 1))
                if later:
                    pe.wait_ge(r32_ok, i)
                reduce_ada(2, m, 6)
                pe.wait_ge(mod_ok, i + 3)
                pe.wait_ge(qkT_ev, i + 1)
                for hd in range(2):
                    pe.matmul(ps[:, 6 + hd, 0:S], qkT[:, 2 + hd, 0:P], qkT[:, hd, :], start=True, stop=True)
                    last = pe.matmul(ps[:, 6 + hd, S:384], qkT[:, 2 + hd, P:S], qkT[:, hd, P:S], start=True, stop=True)
                last.then_inc(sc_done, 1)
                pe.wait_ge(pt_ok, i + 1)
                pe.wait_ge(v_ev, i + 1)
                for hd in range(2):
                    vc = slice(hd * DV, (hd + 1) * DV)
                    pe.matmul(ps[:, 4, vc], PT[:, hd, 0:P], v_t[:, 0, vc], start=True, stop=True)
                    pe.matmul(ps[:, 5, vc], PT[:, hd, P:S], v_t[:, 0, vc], start=True, stop=False)
                    last = pe.matmul(ps[:, 5, vc], PT[:, hd, S:384], v_t[:, 1, vc], start=False, stop=True)
                last.then_inc(pv_done, 1)

            pe.wait_ge(h_ok, 2)
            pair_of_heads(0, 0)
            with pe.Fori(0, PAIRS - 1) as k:
                pair_of_heads(k + 1, k + 1)

            pe.wait_ge(gs_ok, PAIRS)
            pe.wait_ge(rTl_ok, PAIRS - 1)
            for m in range(8):
                if m == 6:
                    pe.wait_ge(rTl_ok, PAIRS)
                by_rows(U_OUT + m, 0, rT_hi, rT_lo, 2 * m, NB, 0, m == 0, m == 7)
                if m == 1:
                    broadcast_gate(0, diag0, 6)
                if m == 3:
                    pe.wait_ge(gbc_ev, 1)
                    broadcast_gate(1, diag1, 6)
                if m == 5:
                    pe.wait_ge(gbc_ev, 2)
                    transpose_r(PAIRS - 1)
                    reduce_ada(6, 0, 4)
                if m == 7:
                    pe.wait_ge(mod_ok, 7)
                    reduce_ada(7, 0, 4)

            transpose_x(1)

            def ff_in(c, m, j):
                if not (isinstance(j, int) and j == 0):
                    pe.wait_ge(fg_ok, j)
                tile(c, m, (0, 1))

            def ff_T(j):
                pe.wait_ge(fg_ok, j + 1)
                if not (isinstance(j, int) and j == 0):
                    pe.wait_ge(fTl_ok, j)
                for c in range(2):
                    for b in range(NB):
                        last = pe.transpose(ps[:, 2, c * S + b * P:c * S + (b + 1) * P],
                                            f_g[:, b, c * P:(c + 1) * P], ident[:, :])
                last.then_inc(fT_done, 1)

            def ff_out(c, m, j, first, last_one):
                pe.wait_ge(fTl_ok, j + 1)
                by_rows(c, m, fT_hi, fT_lo, 0, NB, 4, first, last_one)

            pe.wait_ge(h_ok, 4)
            ff_in(U_FF, 0, 0)
            ff_T(0)

            def ff_two(i, m):
                for o in range(2):
                    c = U_FF + 2 + 3 * o
                    ff_in(c, m, 2 * i + (1 + o))
                    ff_out(c + 2, m, 2 * i + o, isinstance(i, int) and o == 0, False)
                    ff_T(2 * i + (1 + o))
                pe.wait_ge(mod_ok, i + 8)
                reduce_ada(8, m, 3)

            pe.wait_ge(mod_ok, 8)
            ff_two(0, 0)
            with pe.Fori(0, 4) as k:
                ff_two(k + 1, k + 1)
            ff_out(U_FF + 32, 0, FT - 1, False, True)
            pe.wait_ge(mod_ok, 13)
            reduce_ada(13, 0, 3)

            pe.wait_ge(mod_ok, 14)
            transpose_x(2)
            pe.wait_ge(h_ok, 6)
            tile(U_KV, 0, (4, 5))
            tile(U_KV + 2, 0, (6, 7))

            def transpose_kq(n):
                pe.wait_ge(kv_ev, n + 3)
                bank = 4 + 2 * (n % 2)
                for c in range(4):
                    for b in range(NB):
                        last = pe.transpose(ps[:, bank + c // 2, (c % 2) * S + b * P:(c % 2) * S + (b + 1) * P],
                                            qk_t[:, b, c * P:(c + 1) * P], ident[:, :])
                last.then_inc(kqT_done, 1)

            for n in range(2):
                pe.wait_ge(kv_ev, n + 1)
                tile(U_KV + 4 + 2 * n, 0, (4 + 2 * n, 5 + 2 * n))
            transpose_kq(0)
            transpose_kq(1)
            pe.wait_ge(h_ok, 8)
            for n in range(2):
                pe.wait_ge(kqT_ev, n + 1)
                tile(U_Q + 2 * n, 0, (4 + 2 * n, 5 + 2 * n))
            transpose_kq(2)
            transpose_kq(3)
            broadcast_gate(2, diag2, 0)
            broadcast_gate(3, diag3, 2)

            def scores(c):
                if c < 2:
                    pe.wait_ge(gbc_ev, c + 3)
                else:
                    pe.wait_ge(u_ok, c - 1)
                for h in range(2):
                    r = slice(DH * h, DH * (h + 1))
                    o = ps[:, 2 * (c % 2) + h, :]
                    pe.matmul(o[:, 0:S], kT[r, c, 0:P], qT[r, c, :], start=True, stop=True)
                    last = pe.matmul(o[:, S:384], kT[r, c, P:S], qT[r, c, P:S], start=True, stop=True)
                last.then_inc(z_done, 1)

            def tails(c):
                pe.wait_ge(lm_ok, c + 1)
                if c:
                    pe.wait_ge(u_ok, c)
                lm = at_buf(c, 2)
                for h in range(2):
                    o = ps[:, 4 + h, :]
                    pe.matmul(o[:, 0:S], after[:, :], lm[:, h, 0:S], start=True, stop=False)
                    pe.matmul(o[:, P:S], ones[:, :], lm[:, h, S:384], start=False, stop=True)
                    last = pe.matmul(o[:, S:384], after[:, :], lm[:, h, S:384], start=True, stop=True)
                last.then_inc(tail_done, 1)

            def mix_values(c):
                pe.wait_ge(am_ok, c + 1)
                if c >= 2:
                    pe.wait_ge(ol_ok, c - 1)
                a = at_buf(c, 3)
                for h in range(2):
                    o = ps[DH * h:DH * (h + 1), 6 + c % 2, :]
                    vc = slice((2 * c + h) * DH, (2 * c + h + 1) * DH)
                    pe.matmul(o[:, 0:S], v_all[:, 0, vc], a[:, h, 0:S], start=True, stop=False)
                    last = pe.matmul(o[:, P:S], v_all[:, 1, vc], a[:, h, S:384], start=False, stop=True)
                last.then_inc(av_done, 1)

            pe.wait_ge(kqT_ev, 4)
            scores(0)
            scores(1)
            for c in range(KC):
                tails(c)
                if c:
                    mix_values(c - 1)
                if c + 2 < KC:
                    scores(c + 2)
            mix_values(KC - 1)

            pe.wait_ge(ol_ok, KC)
            for t in range(2):
                for h in range(2):
                    c = U_SBO + 2 * t + h
                    landed(c)
                    for q in range(4):
                        kc, cols = 4 * h + q, slice(q * TW, (q + 1) * TW)
                        for b in range(NB):
                            tok = slice(b * P, (b + 1) * P)
                            last = passes(ps[:, 2 * b + t, :], oT_hi[:, kc, tok], oT_lo[:, kc, tok],
                                          w_hi[:, c % RING, cols], w_lo[:, c % RING, cols], kc == 0, kc == KC - 1)
                    last.then_inc(w_used, 1)

            pe.wait_ge(x_ok, 3)
            transpose_x(3)
            pe.wait_ge(h_ok, 10)
            pe.wait_ge(rws_ok, 1)
            for b in range(NB):
                tok = slice(b * P, (b + 1) * P)
                o = ps[:, 4, b * NE:(b + 1) * NE]
                for kc in range(KC):
                    passes(o, hT_hi[:, kc, tok], hT_lo[:, kc, tok], rw_hi[:, kc, :], rw_lo[:, kc, :], kc == 0, False)
                    last = pe.matmul(o, hT_lo[:, kc, tok], rw_lo[:, kc, :], start=False, stop=kc == KC - 1)
            last.then_inc(rt_done, 1)
            for b in range(NB):
                for c in range(KC):
                    last = pe.transpose(ps[:, 2 * b + c // 4, (c % 4) * P:(c % 4 + 1) * P],
                                        h32[:, c, b * P:(b + 1) * P], ident[:, :])
            last.then_inc(hk_done, 1)
            pe.wait_ge(sel_ok, 1)
            pe.matmul(ps[:, 5, 0:8], before[:, :], sel[:, 0, :], start=True, stop=True)
            pe.matmul(ps[:, 5, 8:16], ones[:, :], sel[:, 0, :], start=True, stop=False)
            pe.matmul(ps[:, 5, 8:16], before[:, :], sel[:, 1, :], start=False, stop=True)
            pe.matmul(ps[:, 5, 16:24], ones[:, :], sel[:, 0, :], start=True, stop=False)
            pe.matmul(ps[:, 5, 16:24], ones[:, :], sel[:, 1, :], start=False, stop=True).then_inc(cnt_done, 1)

            def up(c, m, bank):
                for h in range(2):
                    landed(c + h, m)
                    s = (c + h) % RING
                    for t in range(4):
                        kc, cols = 4 * h + t, slice(t * TW, (t + 1) * TW)
                        last = passes(ps[:, bank, :], hg_hi[:, kc, :], hg_lo[:, kc, :], w_hi[:, s, cols],
                                      w_lo[:, s, cols], kc == 0, kc == KC - 1)
                    last.then_inc(w_used, 1)

            def expert_T(nj):
                pe.wait_ge(eg_ok, nj + 1)
                for c in range(4):
                    last = pe.transpose(ps[:, 2, c * P:(c + 1) * P], e_g[:, c * P:(c + 1) * P], ident[:, :])
                last.then_inc(eT_done, 1)

            def down(c, m, nj, first, last_one):
                pe.wait_ge(eTl_ok, nj + 1)
                for h in range(2):
                    by_rows(c + h, m, eT_hi, eT_lo, 2 * h, 1, 4, first and h == 0, last_one and h == 1)

            def step(c, m, nj, first):
                pe.wait_ge(eg_ok, nj)
                up(c, m, 0)
                up(c + 2, m, 1)
                down(c + 4, m, nj - 1, first, False)
                expert_T(nj)

            pe.wait_ge(npass_ok, 1)
            npass = pe.value_load(npass_t[0:1, 0:1], min_val=1, max_val=2)
            pe.wait_ge(hk_ok, 1)
            with pe.Fori(0, npass) as p:
                with pe.Fori(0, NE) as e:
                    n_e = NE * p + e
                    me = ET * n_e
                    pe.wait_ge(hot_ok, n_e + 1)
                    for bank, src in ((0, hk_hi), (2, hk_lo)):
                        for c in range(KC):
                            o = ps[:, bank + c // 4, (c % 4) * P:(c % 4 + 1) * P]
                            for b in range(NB):
                                last = pe.matmul(o, src[:, b, c * P:(c + 1) * P], hot[:, b, :],
                                                 start=b == 0, stop=b == NB - 1)
                    last.then_inc(ga_done, 1)
                    for b in range(NB):
                        last = pe.transpose(ps[:, 6, b * P:(b + 1) * P], hot[:, b, :].bitcast(f32), ident[:, :])
                    last.then_inc(hotT_done, 1)
                    pe.wait_ge(hgh_ok, n_e + 1)
                    pe.wait_ge(hgl_ok, n_e + 1)
                    up(U_MOE, me, 0)
                    up(U_MOE + 2, me, 1)
                    expert_T(me)
                    step(U_MOE + 4, me, me + 1, True)
                    with pe.Fori(0, ET - 2) as k:
                        step(U_MOE + 10, me + k, me + (k + 2), False)
                    down(U_MOE + MOE_U - 2, me, me + (ET - 1), False, True)
                    pe.wait_ge(yl_ok, n_e + 1)
                    pe.wait_ge(hotT_ok, n_e + 1)
                    for b in range(NB):
                        for n in range(2):
                            o, cols = ps[:, 6 - 2 * b + n, :], slice(n * TW, (n + 1) * TW)
                            pe.matmul(o, hotT[:, b * P:(b + 1) * P], y_hi[:, cols], start=True, stop=False)
                            last = pe.matmul(o, hotT[:, b * P:(b + 1) * P], y_lo[:, cols], start=False, stop=True)
                        last.then_inc(scat_done, 1)

        @block.scalar
        def _(act):
            steps = Chain(act, achain)

            def split(c, m=0):
                act.wait_ge(w_in[c % RAW], 32 * (c // RAW + 1) + 32 * m)
                if c >= RING:
                    act.wait_ge(w_used, at(c - RING + 1, m))
                act.activation(w_hi[:, c % RING, :], raw[:, c % RAW, :], ACT.Copy).then_inc(hi_done, 1)

            def root(n):
                for b in range(NB):
                    act.activation((xn0 if n == 0 else xn)[:, b, :], x[:, b, :], ACT.Square,
                                   accum_out=stat[:, b:b + 1]).then_inc(ss_ok, 1)
                act.wait_ge(ms_ok, n + 1)
                act.activation(stat[:, 4:6], stat[:, 2:4], ACT.Sqrt).then_inc(sd_n, 1)

            def modulate(q, shift, n_xT, hT_free):
                act.wait_ge(xT_done, n_xT)
                act.wait_ge(scol_ok, q + 1)
                for c in range(KC):
                    act.activation(h32_at(q)[:, c, :], ps[:, c // 2, (c % 2) * S:(c % 2 + 1) * S], ACT.Identity,
                                   bias=modc[:, shift + c:shift + c + 1], scale=scol[:, q, c:c + 1]).then_inc(h32_ok, 1)
                    if c % 4 == 3:
                        act.wait_ge(h32_ok, KC * q + c + 1)
                        if hT_free and c == 3:
                            act.wait_ge(w_used, hT_free)
                        act.activation(hT_hi[:, c - 3:c + 1, :], h32_at(q)[:, c - 3:c + 1, :], ACT.Copy)\
                           .then_inc(h_hi_ok, 1)

            def gate_out(g, tile, bank):
                act.wait_ge(gbc_done, g + 1)
                act.activation(tile[:, :].rearrange("p (n q) -> p n q", n=2), ps[:, bank:bank + 2, :],
                               ACT.Copy).then_inc(gbc_ev, 1)

            act.wait_ge(vec_ok, 1)
            act.activation(cond[:, :], vec[:, V_C:V_C + KC], ACT.Silu).then_inc(cond_ok, 1)
            act.wait_ge(x_in, 16)
            root(0)
            act.wait_ge(ang_ok, 1)
            act.activation(sin[:, :, :], red, ACT.Sin).then_inc(rt_ok, 1)
            act.activation(cos[:, :, :], tmp_r, ACT.Sin).then_inc(rt_ok, 1)
            split(0)
            split(1)
            modulate(0, MIX0 + SH, 1, 0)

            def high_r(i):
                act.wait_ge(r32_ok, i + 1)
                act.activation(rT_hi[:, ds(i * 4, 4), :], r32, ACT.Copy).then_inc(rTh_ok, 1)

            def pair_of_heads(i, m):
                later = not isinstance(i, int)
                split(2, m)
                split(3, m)
                if later:
                    act.wait_ge(roped, i)
                act.wait_ge(w_used, at(2, m))
                act.activation(qk, ps[:, 0:2, :], ACT.Copy).then_inc(qk_ev, 1)
                if later:
                    high_r(i - 1)
                split(4, m)
                split(5, m)
                if later:
                    act.wait_ge(pv_done, i)
                act.wait_ge(w_used, at(4, m))
                act.activation(v_t, ps[:, 2:4, :], ACT.Copy).then_inc(v_ev, 1)
                act.wait_ge(qkT_done, i + 1)
                if later:
                    act.wait_ge(sc_done, i)
                act.activation(qkT.rearrange("p (n c) s -> p n (c s)", n=2), ps[:, 4:6, :], ACT.Copy)\
                   .then_inc(qkT_ev, 1)
                split(6, m)
                split(7, m)
                if later:
                    act.wait_ge(outT_done, i)
                act.wait_ge(w_used, at(6, m))
                act.activation(gs, ps[:, 0:2, :], ACT.Silu).then_inc(gs_ok, 1)
                act.wait_ge(var_ok, i + 1)
                act.activation(stat[:, 24:28], stat[:, 20:24], ACT.Sqrt).then_inc(sd_ok, 1)

            pair_of_heads(0, 0)
            with act.Fori(0, PAIRS - 1) as k:
                pair_of_heads(k + 1, k + 1)

            split(26)
            split(27)
            gate_out(0, gate_m, 6)
            split(28)
            split(29)
            gate_out(1, gate_f, 6)
            split(30)
            high_r(PAIRS - 1)
            split(31)
            split(32)
            split(33)
            act.wait_ge(x_ok, 1)
            root(1)
            modulate(1, FF0 + SH, 2, U_OUT)

            def ff_act(j, c, m):
                act.wait_ge(w_used, at(c, m))
                if not (isinstance(j, int) and j == 0):
                    act.wait_ge(fg_ok, j)
                act.activation(f_sa, ps[:, 0:2, 0:FW], ACT.Silu).then_inc(fsa_ok, 1)

            def ff_high(j):
                act.wait_ge(fT_done, j + 1)
                act.activation(fT_hi.rearrange("p c s -> p (c s)"), ps[:, 2, :], ACT.Copy).then_inc(fTh_ok, 1)

            ff_act(0, U_FF + 2, 0)
            split(U_FF + 2)
            split(U_FF + 3)
            ff_high(0)

            def ff_two(i, m):
                for o in range(2):
                    c = U_FF + 4 + 3 * o
                    j = 2 * i + (1 + o)
                    split(c, m)
                    ff_act(j, c, m)
                    split(c + 1, m)
                    split(c + 2, m)
                    ff_high(j)

            with act.Fori(0, 5) as k:
                ff_two(k, k)
            split(U_KV + 1)
            split(U_KV + 2)

            act.wait_ge(x_ok, 2)
            root(2)
            modulate(2, KVM + SH, 3, U_KV - 2)

            def tile_out(n, dst):
                act.wait_ge(w_used, U_KV + 2 * n + 2)
                bank = 4 + 2 * (n % 2)
                act.activation(dst, ps[:, bank:bank + 2, :], ACT.Copy).then_inc(kv_ev, 1)

            def kq_out(n):
                act.wait_ge(kqT_done, n + 1)
                bank = 4 + 2 * (n % 2)
                dst = (kT if n < 2 else qT)[:, 4 * (n % 2):4 * (n % 2) + 4, :]
                act.activation(dst.rearrange("p (n c) s -> p n (c s)", n=2), ps[:, bank:bank + 2, :], ACT.Copy,
                               scale=1.0 if n < 2 else DH ** -0.5).then_inc(kqT_ev, 1)

            u = U_KV
            split(u + 3)
            tile_out(0, v_all[:, :, 0:TW])
            split(u + 4)
            split(u + 5)
            tile_out(1, v_all[:, :, TW:D])
            split(u + 6)
            split(u + 7)
            tile_out(2, qk_t)
            split(u + 8)
            split(u + 9)
            kq_out(0)
            tile_out(3, qk_t)
            modulate(3, MIX1 + SH, 3, U_Q)
            kq_out(1)
            split(u + 10)
            split(u + 11)
            act.wait_ge(kqT_done, 2)
            tile_out(4, qk_t)
            split(u + 12)
            split(u + 13)
            kq_out(2)
            tile_out(5, qk_t)
            kq_out(3)
            split(u + 14)
            gate_out(2, gate_m, 0)
            gate_out(3, gate_f, 2)

            def softplus_part(c):
                act.wait_ge(z_done, c + 1)
                if c >= 2:
                    act.wait_ge(a0_ok, c - 1)
                b0 = at_buf(c, 0)
                z = ps[:, 2 * (c % 2):2 * (c % 2) + 2, 0:384]
                steps.link(act.activation(b0, z, ACT.Abs))
                steps.link(act.activation(b0, b0, ACT.Exp, scale=-1.0))
                act.activation(b0, b0, ACT.Ln, bias=ones[:, 0:1]).then_inc(sm_ok, 1)

            def weights(c):
                act.wait_ge(u_ok, c + 1)
                if c >= 2:
                    act.wait_ge(av_done, c - 1)
                act.activation(at_buf(c, 3), at_buf(c, 0), ACT.Exp).then_inc(a0_ok, 1)

            def high_o(c):
                act.wait_ge(av_done, c + 1)
                act.activation(oT_hi[:, c, :], ps[:, 6 + c % 2, 0:S], ACT.Copy).then_inc(oh_ok, 1)

            softplus_part(0)
            softplus_part(1)
            for c in range(KC):
                weights(c)
                if c + 2 < KC:
                    softplus_part(c + 2)
                if c:
                    high_o(c - 1)
            high_o(KC - 1)
            split(u + 15)

            act.dma_start(rw, router[0].rearrange("(t p) e -> p t e", p=P)).then_inc(rw_in, 16)
            act.wait_ge(rw_in, 16)
            act.activation(rw_hi, rw, ACT.Copy).then_inc(rwh_ok, 1)
            act.wait_ge(x_ok, 3)
            root(3)
            modulate(4, FF1 + SH, 4, U_SBO)
            act.wait_ge(dm_ok, 1)
            act.activation(stat[:, 34:36], stat[:, 32:34], ACT.Exp).then_inc(ex_ok, 1)
            act.wait_ge(hk_done, 1)
            act.activation(hk_hi.rearrange("p b (n q) -> p (b n) q", n=2), ps[:, 0:4, :], ACT.Copy)\
               .then_inc(hk_hi_ok, 1)

            def expert_act(nj, c, m):
                act.wait_ge(w_used, at(c, m))
                act.activation(e_sa, ps[:, 0, :], ACT.Silu).then_inc(esa_ok, 1)

            def expert_high(nj):
                act.wait_ge(eT_done, nj + 1)
                act.activation(eT_hi.rearrange("p c s -> p (c s)"), ps[:, 2, :], ACT.Copy).then_inc(eTh_ok, 1)

            act.wait_ge(npass_ok, 1)
            npass = act.value_load(npass_t[0:1, 0:1], min_val=1, max_val=2)
            with act.Fori(0, npass) as p:
                with act.Fori(0, NE) as e:
                    n_e = NE * p + e
                    me = ET * n_e
                    split(U_MOE, me)
                    split(U_MOE + 1, me)
                    act.wait_ge(ga_done, n_e + 1)
                    act.activation(hg_hi.rearrange("p (n c) s -> p n (c s)", n=2), ps[:, 0:2, :], ACT.Copy)\
                       .then_inc(hgh_ok, 1)
                    act.wait_ge(hotT_done, n_e + 1)
                    act.activation(hotT, ps[:, 6, 0:S], ACT.Copy).then_inc(hotT_ok, 1)
                    split(U_MOE + 2, me)
                    split(U_MOE + 3, me)
                    expert_act(me, U_MOE + 2, me)
                    split(U_MOE + 4, me)
                    split(U_MOE + 5, me)
                    expert_high(me)
                    with act.Fori(0, ET - 1) as k:
                        m, nj = me + k, me + (k + 1)
                        split(U_MOE + 6, m)
                        split(U_MOE + 7, m)
                        act.wait_ge(eg_ok, nj)
                        expert_act(nj, U_MOE + 6, m)
                        for n in range(8, 12):
                            split(U_MOE + n, m)
                        expert_high(nj)
                    act.wait_ge(w_used, at(U_MOE + MOE_U, me))
                    act.activation(y_hi.rearrange("p (n q) -> p n q", n=2), ps[:, 4:6, :], ACT.Copy).then_inc(yh_ok, 1)

            act.wait_ge(x_ok, 4)
            root(4)

        @block.vector
        def _(dve):
            steps = Chain(dve, vchain)
            v = nc.vector

            def split(c, m=0):
                dve.wait_ge(hi_done, at(c + 1, m))
                v.tensor_tensor(w_lo[:, c % RING, :], raw[:, c % RAW, :], w_hi[:, c % RING, :].bitcast(f32),
                                ALU.subtract).then_inc(lo_done, 1)

            def ada_tile(t, k=0):
                a = acc[:, t % 2, :]
                if t >= 2:
                    dve.wait_ge(acc_red, t // 2 + k)
                for h in range(2):
                    dve.wait_ge(ada_in[h], 16 * (t + 1) + 32 * k)
                    for n in range(4):
                        kc = 4 * h + n
                        w = ada[:, h, n * TW:(n + 1) * TW]
                        if kc == 0:
                            ins = v.tensor_scalar(a, w, cond[:, 0:1], None, ALU.mult)
                        else:
                            ins = v.scalar_tensor_tensor(a, w, cond[:, kc:kc + 1], a, ALU.mult, ALU.add)
                        if n < 3:
                            steps.link(ins)
                        else:
                            ins.then_inc(ada_used, 1)
                            if h == 0:
                                dve.wait_ge(ada_used, 2 * t + 1 + 4 * k)

            def mod_out(pair, k, bank):
                dve.wait_ge(acc_red, pair + 1 + k)
                if isinstance(k, int):
                    col = slice(8 * (pair + k), 8 * (pair + k) + 8)
                else:
                    col = ds(8 * k + 8 * pair, 8)
                v.tensor_tensor(modc[:, col], ps[:, bank, 0:8], vec[:, col], ALU.add).then_inc(mod_ok, 1)

            def scale_col(q, at_scale, gain, pairs):
                dve.wait_ge(mod_ok, pairs)
                v.scalar_tensor_tensor(scol[:, q, :], modc[:, at_scale:at_scale + KC], 1.0, vec[:, gain:gain + KC],
                                       ALU.add, ALU.mult).then_inc(scol_ok, 1)

            def root(n):
                dve.wait_ge(ss_ok, 2 * n + 2)
                v.tensor_scalar(stat[:, 2:4], stat[:, 0:2], 1.0 / D, EPS, ALU.mult, ALU.add).then_inc(ms_ok, 1)
                dve.wait_ge(sd_n, n + 1)
                steps.link(v.reciprocal(stat[:, 6:8], stat[:, 4:6]))
                if n < 4:
                    for b in range(NB):
                        v.tensor_scalar((xn0 if n == 0 else xn)[:, b, :], x[:, b, :], stat[:, 6 + b:7 + b], None,
                                        ALU.mult).then_inc(xn_ok, 1)

            def low_h(q):
                for h in range(2):
                    dve.wait_ge(h_hi_ok, 2 * q + h + 1)
                    v.tensor_tensor(hT_lo[:, 4 * h:4 * h + 4, :], h32_at(q)[:, 4 * h:4 * h + 4, :],
                                    hT_hi[:, 4 * h:4 * h + 4, :].bitcast(f32), ALU.subtract).then_inc(h_ok, 1)

            def diagonal(g, dg, col):
                v.tensor_tensor(dg, ident[:, :].unsqueeze(1).to_broadcast([P, KC, P]),
                                modc[:, col:col + KC].unsqueeze(2).to_broadcast([P, KC, P]),
                                ALU.mult).then_inc(diag_ok, 1)

            def add_gated(bank, gate, tmp):
                for b in range(NB):
                    y = ps[:, bank + 2 * b:bank + 2 * b + 2, :]
                    t = tmp[:, b, :].rearrange("p (n q) -> p n q", n=2)
                    steps.link(v.tensor_tensor(t, y, gate[:, :].rearrange("p (n q) -> p n q", n=2), ALU.mult))
                    ins = v.tensor_tensor(x[:, b, :], x[:, b, :], tmp[:, b, :], ALU.add)
                    if b == NB - 1:
                        ins.then_inc(x_ok, 1)

            dve.wait_ge(vecT_done, 1)
            v.tensor_copy(vec[:, :], ps[:, 4, 0:176]).then_inc(vec_ok, 1)
            dve.wait_ge(pos_in, 32)
            steps.link(v.tensor_copy(stat[:, 8:10], pos_i[:, :]))
            for b in range(NB):
                ins = v.tensor_scalar(ang[:, b, :], freq, stat[:, 8 + b:9 + b], None, ALU.mult)
            steps.link(ins)
            big = 1.5 * 2.0 ** 23
            steps.link(v.tensor_scalar(kk, ang, float(1 / (2 * np.pi)), big, ALU.mult, ALU.add))
            steps.link(v.tensor_scalar(kk, kk, big, None, ALU.subtract))
            p1 = 6.28125
            p2 = float(np.float32(np.round((2 * np.pi - p1) * 2 ** 20) / 2 ** 20))
            p3 = float(2 * np.pi - p1 - p2)
            steps.link(v.scalar_tensor_tensor(red, kk, -p1, ang, ALU.mult, ALU.add))
            steps.link(v.scalar_tensor_tensor(red, kk, -p2, red, ALU.mult, ALU.add))
            steps.link(v.scalar_tensor_tensor(red, kk, -p3, red, ALU.mult, ALU.add))
            pi = float(np.nextafter(np.float32(np.pi), np.float32(0)))
            steps.link(v.tensor_scalar(red, red, pi, -pi, ALU.min, ALU.max))
            steps.link(v.scalar_tensor_tensor(tmp_r, red, -1.0, red, ALU.mult, ALU.max))
            v.tensor_scalar(tmp_r, tmp_r, -1.0, float(np.pi / 2), ALU.mult, ALU.add).then_inc(ang_ok, 1)

            dve.wait_ge(cond_ok, 1)
            ada_tile(0)
            root(0)
            ada_tile(1)
            mod_out(0, 0, 4)
            split(0)
            split(1)
            ada_tile(2)
            ada_tile(3)
            mod_out(1, 0, 4)
            scale_col(0, MIX0 + SC, V_MIX, 2)
            low_h(0)

            def low_r(i):
                dve.wait_ge(outT_done, i + 1)
                for c in range(4):
                    col = V_GN + 4 * i + c
                    sc_ap = vec[:, col:col + 1] if isinstance(i, int) else vec[:, ds(4 * i + (V_GN + c), 1)]
                    ins = v.tensor_scalar(r32[:, c, :], ps[:, 6 + c // 2, (c % 2) * S:(c % 2 + 1) * S], sc_ap, None,
                                          ALU.mult)
                ins.then_inc(r32_ok, 1)
                dve.wait_ge(rTh_ok, i + 1)
                v.tensor_tensor(rT_lo[:, ds(i * 4, 4), :], r32, rT_hi[:, ds(i * 4, 4), :].bitcast(f32),
                                ALU.subtract).then_inc(rTl_ok, 1)

            def pair_of_heads(i, m):
                later = not isinstance(i, int)
                split(2, m)
                split(3, m)
                if later:
                    low_r(i - 1)
                ada_tile(4, m)
                split(4, m)
                split(5, m)
                ada_tile(5, m)
                split(6, m)
                split(7, m)
                mod_out(2, m, 6)
                dve.wait_ge(sc_done, i + 1)
                dve.wait_ge(decay_in, 16 * i + 16)
                v.tensor_tensor(PT, ps[:, 6:8, 0:384], decay, ALU.mult).then_inc(pt_ok, 1)
                dve.wait_ge(pv_done, i + 1)
                for b in range(NB):
                    for hd in range(2):
                        n = 2 * b + hd
                        ins = v.bn_stats(stat[:, 40 + 6 * n:46 + 6 * n],
                                         ps[:, 4 + b, hd * DV:(hd + 1) * DV])
                steps.link(ins)
                v.memset(stat[:, 19:20], 0.0)
                for n in range(4):
                    ins = v.bn_aggr(mv[:, n, :], stat[:, 40 + 6 * n:46 + 6 * n])
                steps.link(ins)
                v.tensor_scalar(stat[:, 20:24], mv[:, :, 1], EPS, None, ALU.add).then_inc(var_ok, 1)
                dve.wait_ge(gs_ok, i + 1)
                for n in range(4):
                    b, hd = n // 2, n % 2
                    cols = slice(hd * DV, (hd + 1) * DV)
                    ins = v.scalar_tensor_tensor(gs[:, b, cols], ps[:, 4 + b, cols], mv[:, n, 0:1], gs[:, b, cols],
                                                 ALU.subtract, ALU.mult)
                steps.link(ins)
                dve.wait_ge(sd_ok, i + 1)
                steps.link(v.reciprocal(stat[:, 28:32], stat[:, 24:28]))
                for n in range(4):
                    b, hd = n // 2, n % 2
                    cols = slice(hd * DV, (hd + 1) * DV)
                    ins = v.tensor_scalar(gs[:, b, cols], gs[:, b, cols], stat[:, 28 + n:29 + n], None, ALU.mult)
                ins.then_inc(r_ok, 1)

            pair_of_heads(0, 0)
            with dve.Fori(0, PAIRS - 1) as k:
                steps.enter(k, PAIR_STEPS)
                pair_of_heads(k + 1, k + 1)
                steps.leave(PAIRS - 1)

            dve.wait_ge(roped, PAIRS)
            dve.wait_ge(qkT_done, PAIRS)
            diagonal(0, diag0, MIX0 + G)
            diagonal(1, diag1, FF0 + G)
            split(26)
            split(27)
            ada_tile(12)
            split(28)
            split(29)
            ada_tile(13)
            split(30)
            low_r(PAIRS - 1)
            mod_out(6, 0, 4)
            split(31)
            ada_tile(14)
            ada_tile(15)
            split(32)
            split(33)
            dve.wait_ge(w_used, U_FF)
            dve.wait_ge(gbc_ev, 2)
            add_gated(0, gate_m, f_tmp)
            mod_out(7, 0, 4)
            root(1)
            scale_col(1, FF0 + SC, V_FF, 6)
            low_h(1)

            def ff_product(j):
                if not (isinstance(j, int) and j == 0):
                    dve.wait_ge(fT_done, j)
                dve.wait_ge(fsa_ok, j + 1)
                v.tensor_tensor(f_g, ps[:, 0:2, FW:2 * FW], f_sa, ALU.mult).then_inc(fg_ok, 1)

            def ff_low(j):
                dve.wait_ge(fTh_ok, j + 1)
                v.tensor_tensor(fT_lo.rearrange("p c s -> p (c s)"), ps[:, 2, :],
                                fT_hi.rearrange("p c s -> p (c s)").bitcast(f32), ALU.subtract).then_inc(fTl_ok, 1)

            ff_product(0)
            split(U_FF + 2)
            split(U_FF + 3)
            ff_low(0)

            def ff_two(i, m):
                for o in range(2):
                    c = U_FF + 4 + 3 * o
                    j = 2 * i + (1 + o)
                    split(c, m)
                    ff_product(j)
                    split(c + 1, m)
                    split(c + 2, m)
                    ff_low(j)
                    if o == 0 and not isinstance(i, int):
                        mod_out(7, m, 3)
                    ada_tile(16 + o, m)

            ff_two(0, 0)
            with dve.Fori(0, 4) as k:
                steps.enter(k, 12)
                ff_two(k + 1, k + 1)
                steps.leave(4)
            mod_out(12, 0, 3)
            ada_tile(26)
            ada_tile(27)
            split(U_KV + 1)
            split(U_KV + 2)
            mod_out(13, 0, 3)
            dve.wait_ge(w_used, U_KV)
            add_gated(4, gate_f, f_tmp)

            root(2)
            scale_col(2, KVM + SC, V_KVN, 8)
            scale_col(3, MIX1 + SC, V_MIX + KC, 10)
            low_h(2)
            u = U_KV
            for n in range(3, 10):
                split(u + n)
            low_h(3)
            for n in range(10, 15):
                split(u + n)
            dve.wait_ge(kqT_done, 4)
            diagonal(2, diag2, MIX1 + G)
            diagonal(3, diag3, FF1 + G)

            mask = causal[:, :].unsqueeze(1).to_broadcast([P, 2, 384])

            def softplus(c):
                dve.wait_ge(sm_ok, c + 1)
                z = ps[:, 2 * (c % 2):2 * (c % 2) + 2, 0:384]
                b0, b1, b2 = (at_buf(c, n) for n in range(3))
                steps.link(v.scalar_tensor_tensor(b1, z, 0.0, b0, ALU.max, ALU.add))
                v.tensor_tensor(b2, b1, mask, ALU.mult).then_inc(lm_ok, 1)
                steps.link(v.tensor_tensor(b0, z, b1, ALU.subtract))

            def log_weights(c):
                dve.wait_ge(tail_done, c + 1)
                v.tensor_tensor(at_buf(c, 0), at_buf(c, 0), ps[:, 4:6, 0:384], ALU.subtract).then_inc(u_ok, 1)

            def low_o(c):
                dve.wait_ge(oh_ok, c + 1)
                v.tensor_tensor(oT_lo[:, c, :], ps[:, 6 + c % 2, 0:S], oT_hi[:, c, :].bitcast(f32),
                                ALU.subtract).then_inc(ol_ok, 1)

            softplus(0)
            for c in range(KC):
                if c + 1 < KC and c > 0:
                    softplus(c + 1)
                log_weights(c)
                if c == 0:
                    softplus(1)
                if c:
                    low_o(c - 1)
            low_o(KC - 1)
            split(u + 15)
            dve.wait_ge(rwh_ok, 1)
            v.tensor_tensor(rw_lo, rw, rw_hi.bitcast(f32), ALU.subtract).then_inc(rws_ok, 1)
            dve.wait_ge(w_used, U_MOE)
            add_gated(0, gate_m, f_tmp)
            root(3)
            scale_col(4, FF1 + SC, V_FF + KC, 13)
            low_h(4)

            dve.wait_ge(rt_done, 1)
            steps.link(v.tensor_copy(logit, ps[:, 4, 0:2 * NE].rearrange("p (b e) -> p b e", b=NB)))
            for b in range(NB):
                ins = v.max(mx[:, b, :], logit[:, b, :])
            steps.link(ins)
            v.tensor_tensor(stat[:, 32:34], mx[:, :, 1], mx[:, :, 0], ALU.subtract).then_inc(dm_ok, 1)
            for b in range(NB):
                ins = v.max_index(ridx[:, b, :], mx[:, b, :], logit[:, b, :])
            steps.link(ins)
            steps.link(v.tensor_copy(stat[:, 36:40].rearrange("p (b k) -> p b k", b=NB), ridx[:, :, 0:2]))
            for b in range(NB):
                for k2, oh in enumerate((oh1, oh2)):
                    ins = v.tensor_scalar(oh[:, b, :], slot_no[:, 0:NE], stat[:, 36 + 2 * b + k2:37 + 2 * b + k2], None,
                                          ALU.is_equal)
            steps.link(ins)
            v.tensor_tensor(sel, oh1, oh2, ALU.add).then_inc(sel_ok, 1)
            dve.wait_ge(ex_ok, 1)
            steps.link(v.tensor_scalar(stat[:, 10:12], stat[:, 34:36], 1.0, None, ALU.add))
            steps.link(v.reciprocal(stat[:, 12:14], stat[:, 10:12]))
            steps.link(v.tensor_tensor(stat[:, 14:16], stat[:, 12:14], stat[:, 34:36], ALU.mult))
            for b in range(NB):
                ins = v.tensor_scalar(gate_e[:, b, :], oh1[:, b, :], stat[:, 12 + b:13 + b], None, ALU.mult)
            steps.link(ins)
            for b in range(NB):
                ins = v.scalar_tensor_tensor(gate_e[:, b, :], oh2[:, b, :], stat[:, 14 + b:15 + b], gate_e[:, b, :],
                                             ALU.mult, ALU.add)
            steps.link(ins)
            dve.wait_ge(hk_hi_ok, 1)
            v.tensor_tensor(hk_lo.rearrange("p b (n q) -> p (b n) q", n=2), ps[:, 0:4, :],
                            hk_hi.rearrange("p b (n q) -> p (b n) q", n=2).bitcast(f32), ALU.subtract).then_inc(hk_ok, 1)
            dve.wait_ge(cnt_done, 1)
            v.tensor_copy(slot, ps[:, 5, 0:2 * NE].rearrange("p (b e) -> p b e", b=NB))
            steps.link(v.tensor_reduce(stat[:, 16:17], ps[:, 5, 2 * NE:3 * NE], AX.X, ALU.max))
            v.tensor_scalar(npass_t[:, :], stat[:, 16:17], float(P), 1.0, ALU.is_gt, ALU.add).then_inc(npass_ok, 1)

            def expert_product(nj):
                dve.wait_ge(esa_ok, nj + 1)
                v.tensor_tensor(e_g, ps[:, 1, :], e_sa, ALU.mult).then_inc(eg_ok, 1)

            def expert_low(nj):
                dve.wait_ge(eTh_ok, nj + 1)
                v.tensor_tensor(eT_lo.rearrange("p c s -> p (c s)"), ps[:, 2, :],
                                eT_hi.rearrange("p c s -> p (c s)").bitcast(f32), ALU.subtract).then_inc(eTl_ok, 1)

            dve.wait_ge(npass_ok, 1)
            npass = dve.value_load(npass_t[0:1, 0:1], min_val=1, max_val=2)
            dve.wait_ge(yz_ok, 1)
            with dve.Fori(0, npass) as p:
                steps.enter(p, 1 + NE)
                with dve.Fori(0, NE) as e:
                    steps.enter(e, 1)
                    n_e = NE * p + e
                    me = ET * n_e
                    for b in range(NB):
                        ins = v.tensor_scalar(hot[:, b, :], slot_no[:, :], slot[:, b, ds(e, 1)], sel[:, b, ds(e, 1)],
                                              ALU.is_equal, ALU.mult)
                    ins.then_inc(hot_ok, 1)
                    split(U_MOE, me)
                    split(U_MOE + 1, me)
                    dve.wait_ge(ga_done, n_e + 1)
                    v.tensor_copy(hg_lo.rearrange("p (n c) s -> p n (c s)", n=2), ps[:, 2:4, :]).then_inc(hgl_ok, 1)
                    split(U_MOE + 2, me)
                    split(U_MOE + 3, me)
                    dve.wait_ge(w_used, at(U_MOE + 4, me))
                    expert_product(me)
                    split(U_MOE + 4, me)
                    split(U_MOE + 5, me)
                    expert_low(me)
                    with dve.Fori(0, ET - 1) as k:
                        m, nj = me + k, me + (k + 1)
                        split(U_MOE + 6, m)
                        split(U_MOE + 7, m)
                        split(U_MOE + 8, m)
                        dve.wait_ge(w_used, at(U_MOE + 8, m))
                        dve.wait_ge(eT_done, nj)
                        expert_product(nj)
                        for n in range(9, 12):
                            split(U_MOE + n, m)
                        expert_low(nj)
                    dve.wait_ge(yh_ok, n_e + 1)
                    v.tensor_tensor(y_lo.rearrange("p (n q) -> p n q", n=2), ps[:, 4:6, :],
                                    y_hi.rearrange("p (n q) -> p n q", n=2).bitcast(f32), ALU.subtract).then_inc(yl_ok, 1)
                    for b in range(NB):
                        dve.wait_ge(scat_done, NB * n_e + b + 1)
                        ya = y_acc[:, b, :].rearrange("p (n q) -> p n q", n=2)
                        ins = v.scalar_tensor_tensor(ya, ps[:, 6 - 2 * b:8 - 2 * b, :], gate_e[:, b, ds(e, 1)], ya,
                                                     ALU.mult, ALU.add)
                    steps.link(ins)
                    steps.leave(NE)
                steps.link(v.tensor_scalar(slot, slot, -float(P), None, ALU.add))
                steps.leave(npass)

            for b in range(NB):
                steps.link(v.tensor_tensor(y_acc[:, b, :], y_acc[:, b, :], gate_f[:, :], ALU.mult))
                ins = v.tensor_tensor(x[:, b, :], x[:, b, :], y_acc[:, b, :], ALU.add)
            ins.then_inc(x_ok, 1)
            root(4)
            dve.wait_ge(fnorm_in, 16)
            for b in range(NB):
                v.scalar_tensor_tensor(x[:, b, :], x[:, b, :], stat[:, 6 + b:7 + b], fnorm, ALU.mult,
                                       ALU.mult).then_inc(o_ok, 1)


class Chain:

    def __init__(self, engine, semaphore):
        self.engine, self.semaphore, self.n, self.base, self.kept = engine, semaphore, 0, 0, []

    def link(self, instruction):
        self.n += 1
        instruction.then_inc(self.semaphore, 1)
        self.engine.wait_ge(self.semaphore, self.base + self.n)

    def enter(self, register, per_turn):
        self.kept.append((self.base, self.n, per_turn))
        self.base = self.base + register * per_turn

    def leave(self, turns):
        base, n, per_turn = self.kept.pop()
        assert self.n - n == per_turn, (self.n - n, per_turn)
        self.base, self.n = (base, n + turns * per_turn) if isinstance(turns, int) else (base + turns * per_turn, n)


_INS = ["x", "c", "positions", "ada_w", "ada_b", "norm_mix", "norm_ff", "ret_w_in", "ret_gn", "ret_w_out",
        "kv_ada_w", "kv_ada_b", "kv_norm", "kv_w", "sb_w_q", "sb_w_out", "ff_w_in", "ff_w_out", "moe_router",
        "moe_w_in", "moe_w_out", "final_norm"]


def _constants():
    log_gamma = np.log(1.0 - np.exp2(-5.0 - np.arange(RET_HEADS)))
    m, n = np.arange(S)[:, None], np.arange(S)[None, :]
    table = np.exp(np.abs(m - n)[None] * log_gamma[:, None, None]) * (m // CHUNK <= n // CHUNK) * DK ** -0.5
    both = np.concatenate([table[:, :P, :], table[:, P:, P:]], axis=2)
    decay = both.reshape(PAIRS, 2, P, 384).transpose(0, 2, 1, 3).reshape(PAIRS * P, 768)
    freq = 10000.0 ** (-np.arange(0, DK, 2) / DK)
    return decay.astype(np.float32), freq.astype(np.float32)[None, :]


def kernel(**inputs):
    import concourse.bacc as bacc
    from concourse.bass_utils import run_bass_kernel_spmd

    nc = bacc.Bacc("TRN2", target_bir_lowering=False, num_devices=1, dynamic_dma_scratch_size=DMA_SCRATCH)
    decay, freq = _constants()
    given = {name: inputs[name] for name in _INS} | {"decay_table": decay, "frequencies": freq}
    arrays, args = {}, []
    for name, value in given.items():
        a = np.ascontiguousarray(value)
        arrays[f"in_{name}"] = a
        args.append(nc.dram_tensor(f"in_{name}", a.shape, mybir.dt.from_np(a.dtype), kind="ExternalInput").ap())
    out = nc.dram_tensor("out_x", (1, S, D), mybir.dt.float32, kind="ExternalOutput").ap()
    trunk(nc, *args, out)
    r = run_bass_kernel_spmd(nc, [arrays], core_ids=[0])
    return r.results[0]["out_x"]
```

```python
from contextlib import ExitStack

import numpy as np
import concourse.bass as bass
from concourse import mybir

P = 128
S = 256
D = 1024
NB = S // P
KC = D // P
TW = 512
RET_HEADS, DK, DV, CHUNK = 8, 128, 256, 64
PAIRS = RET_HEADS // 2
SB_HEADS, DH = 16, 64
FF = 2816
FW = 256
FT = FF // FW
NE, FE = 8, 3584
ET = FE // TW
EPS = 1e-6
RAW, RING = 6, 3
DMA_SCRATCH = 2048
PAIR_STEPS = 5
HALF = 2048

U_RET = 0
U_OUT = U_RET + 6 * PAIRS
U_FF = U_OUT + 8
U_KV = U_FF + 3 * FT
U_Q = U_KV + 8
U_SBO = U_Q + 4
U_MOE = U_SBO + 4
MOE_U = 6 * ET

SH, SC, G = 0, 8, 16
MIX0, FF0, KVM, MIX1, FF1 = 0, 24, 48, 64, 88
V_MIX, V_FF, V_KVN, V_GN, V_C = 112, 128, 144, 152, 168


def trunk(nc, x_d, c_d, pos_d, ada_w, ada_b, norm_mix, norm_ff, ret_w_in, ret_gn, ret_w_out, kv_ada_w,
          kv_ada_b, kv_norm, kv_w, sb_w_q, sb_w_out, ff_w_in, ff_w_out, router, moe_w_in, moe_w_out,
          final_norm, decay_d, freq_d, out_d):
    f32, f32r, i32, u32 = mybir.dt.float32, mybir.dt.float32r, mybir.dt.int32, mybir.dt.uint32
    ALU, ACT, AX = mybir.AluOpType, mybir.ActivationFunctionType, mybir.AxisListType
    ds = bass.ds

    ctx = ExitStack()
    with ctx:
        def sb(name, shape, dt=f32):
            return ctx.enter_context(nc.sbuf_tensor(name, shape, dt))

        def sem(name):
            return ctx.enter_context(nc.semaphore(name))

        raw = sb("raw", [P, RAW, HALF])
        w_hi = sb("w_hi", [P, RING, HALF], f32r)
        w_lo = sb("w_lo", [P, RING, HALF], f32r)
        x = sb("x", [P, NB, D])
        hT_hi = sb("hT_hi", [P, KC, S], f32r)
        hT_lo = sb("hT_lo", [P, KC, S], f32r)
        ada = sb("ada", [P, 2, HALF])
        acc = sb("acc", [P, 2, TW])
        gate_m = sb("gate_m", [P, D])
        gate_f = sb("gate_f", [P, D])
        RA = sb("RA", [P, 8192], f32r)
        FA = sb("FA", [P, 9216])
        ident = sb("ident", [P, P])
        ones = sb("ones", [P, P])
        before = sb("before", [P, P])
        after = sb("after", [P, P])
        slot_no = sb("slot_no", [P, P])
        causal = sb("causal", [P, P])
        vec = sb("vec", [P, 176])
        modc = sb("modc", [P, 112])
        cond = sb("cond", [P, KC])
        scol = sb("scol", [P, 5, KC])
        cos, sin = (gate_m[:, n * P:(n + 1) * P].rearrange("p (b f) -> p b f", b=NB) for n in range(2))
        stat = sb("stat", [P, 64])
        eps = sb("eps", [P, 1])
        tsum = sb("tsum", [P, 4])
        mv = sb("mv", [P, 4, 2])
        ridx = sb("ridx", [P, NB, 8], u32)
        npass_t = sb("npass_t", [P, 1], i32)
        pos_i = sb("pos_i", [P, NB], i32)
        ps = ctx.enter_context(nc.psum_tensor("ps", [P, 8, 512], f32))

        def fa(off, *shape):
            n = int(np.prod(shape))
            v = FA[:, off:off + n]
            if len(shape) == 1:
                return v
            names = "abcd"[:len(shape)]
            return v.rearrange(f"p ({' '.join(names)}) -> p {' '.join(names)}", **dict(zip(names, shape)))

        def ra(off, *shape):
            n = int(np.prod(shape))
            v = RA[:, off:off + n]
            if len(shape) == 1:
                return v
            names = "abcd"[:len(shape)]
            return v.rearrange(f"p ({' '.join(names)}) -> p {' '.join(names)}", **dict(zip(names, shape)))

        qk = fa(0, NB, 512)
        qkr = fa(1024, NB, 512)
        v_t = fa(2048, NB, 512)
        gs = fa(3072, NB, 512)
        r32 = fa(4096, 4, S)
        qkT = fa(5120, 4, S)
        PT = fa(6144, 2, 384)
        decay = fa(6912, 2, 384)
        rope_t = fa(7680, 2, 512)
        rT_hi = ra(0, 16, S)
        rT_lo = ra(4096, 16, S)
        ada_first = raw[:, 4:6, :]
        diag0, diag1 = fa(1024, KC, P), fa(0, KC, P)
        xn = fa(6144, NB, D)
        xn0 = fa(2048, NB, D)
        h32 = fa(6144, KC, S)
        h32_0 = fa(2048, KC, S)

        def h32_at(q):
            return h32_0 if q == 0 else h32

        f_sa = fa(0, NB, FW)
        f_g = fa(512, NB, FW)
        f_tmp = fa(1024, NB, D)
        fT_hi = ra(0, 2, S)
        fT_lo = ra(512, 2, S)
        v_all = fa(0, NB, D)
        qT = fa(2048, KC, S)
        kT = fa(4096, KC, S)
        qk_t = (fa(8192, NB, 512), fa(6144, NB, 512))
        hq_hi = ra(0, KC, S)
        hq_lo = ra(2048, KC, S)
        ada_flat = ada[:, :, :].rearrange("p a b -> p (a b)")
        diag2 = diag3 = ada_flat[:, 3072:4096].rearrange("p (c q) -> p c q", c=KC)
        oT_hi = ra(0, KC, S)
        oT_lo = ra(2048, KC, S)

        def at_buf(c, n):
            src = (FA[:, 6144:9216] if c % 2 == 0 else ada_flat[:, 0:3072])
            off = (c // 2 % 2) * 1536 + n * 768
            return src[:, off:off + 768].rearrange("p (h t) -> p h t", h=2)

        def on_diagonal(buf):
            return buf.rearrange("p h (t q) -> p h t q", q=P)[:, :, 0:3:2, :]

        y32 = fa(0, D)
        e_sa = fa(2048, TW)
        e_g = fa(2560, TW)
        ht = fa(5120, D)
        hk_hi = hT_hi[:, :, :].rearrange("p c s -> p (c s)").rearrange("p (b d) -> p b d", b=NB)
        hk_lo = hT_lo[:, :, :].rearrange("p c s -> p (c s)").rearrange("p (b d) -> p b d", b=NB)
        hg_hi = ra(0, KC, P)
        hg_lo = ra(1024, KC, P)
        eT_hi = ra(2048, 4, P)
        eT_lo = ra(2560, 4, P)
        hot = ra(3072, NB, P)
        hotT = ra(3328, S)
        y_hi = ra(3584, D)
        y_lo = ra(4608, D)
        logit, gate_e, sel, slot, oh1, oh2, mx = (fa(3072 + 16 * n, NB, NE) for n in range(7))
        rw = fa(3328, KC, NE)
        freq = FA[:, 0:64]
        ang, red, kk, tmp_r = (fa(64 + 128 * n, NB, 64) for n in range(4))
        rows = fa(1024, 2, P)
        fnorm = fa(4096, D)

        small_in = sem("small_in"); pos_in = sem("pos_in"); x_in = sem("x_in"); rw_in = sem("rw_in")
        fnorm_in = sem("fnorm_in"); ang_ok = sem("ang_ok"); rs_ok = sem("rs_ok")
        const_ok = sem("const_ok"); pchain = sem("pchain")
        vecT_done = sem("vecT_done"); vec_ok = sem("vec_ok"); cond_ok = sem("cond_ok")
        w_in = [sem(f"w_in{n}") for n in range(RAW)]
        hi_done = sem("hi_done"); lo_done = sem("lo_done"); w_used = sem("w_used")
        ada_in = [sem("ada_in0"), sem("ada_in1")]
        ada_step = sem("ada_step"); first_in = sem("first_in"); first_done = sem("first_done")
        first_ok = sem("first_ok")
        acc_red = sem("acc_red"); mod_ok = sem("mod_ok")
        vchain = sem("vchain"); achain = sem("achain")
        decay_in = sem("decay_in")
        ss_ok = sem("ss_ok"); rt_ok = sem("rt_ok"); xn_ok = sem("xn_ok")
        xT_done = sem("xT_done"); h32a_ok = sem("h32a_ok"); h32b_ok = sem("h32b_ok"); h_hi_ok = sem("h_hi_ok"); h_ok = sem("h_ok")
        scol_ok = sem("scol_ok")
        qk_ev = sem("qk_ev"); v_ev = sem("v_ev"); gs_ok = sem("gs_ok"); roped = sem("roped")
        qkT_done = sem("qkT_done"); qkT_ev = sem("qkT_ev"); sc_done = sem("sc_done"); pt_ok = sem("pt_ok")
        pv_done = sem("pv_done"); var_ok = sem("var_ok"); sd_ok = sem("sd_ok"); r_ok = sem("r_ok")
        outT_done = sem("outT_done"); r32_ok = sem("r32_ok"); rTh_ok = sem("rTh_ok"); rTl_ok = sem("rTl_ok")
        diag_ok = sem("diag_ok"); gbc_done = sem("gbc_done"); gbc_ev = sem("gbc_ev")
        x_ok = sem("x_ok")
        fsa_ok = sem("fsa_ok"); fg_ok = sem("fg_ok"); fT_done = sem("fT_done")
        fTh_ok = sem("fTh_ok"); fTl_ok = sem("fTl_ok")
        kv_ev = sem("kv_ev"); kqT_done = sem("kqT_done"); kqT_ev = sem("kqT_ev")
        z_done = sem("z_done"); sm_ok = sem("sm_ok"); lm_ok = sem("lm_ok"); e_ok = sem("e_ok"); z_used = sem("z_used")
        tail_done = sem("tail_done"); u_ok = sem("u_ok"); a0_ok = sem("a0_ok"); am_ok = sem("am_ok")
        av_done = sem("av_done"); oh_ok = sem("oh_ok"); ol_ok = sem("ol_ok")
        rt_done = sem("rt_done"); dm_ok = sem("dm_ok"); ex_ok = sem("ex_ok")
        sel_ok = sem("sel_ok"); cnt_done = sem("cnt_done"); npass_ok = sem("npass_ok")
        hk_done = sem("hk_done"); hk_hi_ok = sem("hk_hi_ok"); hk_ok = sem("hk_ok"); yg_ok = sem("yg_ok")
        hot_ok = sem("hot_ok"); ga_done = sem("ga_done"); hgh_ok = sem("hgh_ok"); hgl_ok = sem("hgl_ok")
        hgT_done = sem("hgT_done"); ht_ok = sem("ht_ok"); yacc_ok = sem("yacc_ok")
        hotT_done = sem("hotT_done"); hotT_ok = sem("hotT_ok")
        esa_ok = sem("esa_ok"); eg_ok = sem("eg_ok"); eT_done = sem("eT_done")
        eTh_ok = sem("eTh_ok"); eTl_ok = sem("eTl_ok"); yh_ok = sem("yh_ok")
        yl_ok = sem("yl_ok"); scat_done = sem("scat_done")
        o_ok = sem("o_ok"); stored = sem("stored")

        block = ctx.enter_context(nc.Block())

        def before_half(c, m=0):
            return 2 * c + 2 * RAW * m

        @block.sync
        def _(sp):
            def free(c, m=0):
                if c >= RAW:
                    sp.wait_ge(lo_done, before_half(c - RAW + 1, m))

            def cols_of(w, row, col, n):
                return w[ds(row, 4 * P), ds(col, n)].rearrange("(t p) n -> p t n", p=P)

            def slot4(c, lo, n):
                return raw[:, c % RAW, :].rearrange("p (t n) -> p t n", t=4)[:, :, lo:lo + n]

            def load_tile(c, m, w, row, col):
                for h in range(2):
                    load_half(c + h, m, w, row + h * 4 * P, col)

            def load_half(c, m, w, row, col):
                free(c, m)
                sp.dma_start(slot4(c, 0, TW), cols_of(w, row, col, TW)).then_inc(w_in[c % RAW], 32)

            def load_half2(c, m, w, row, col_a, col_b):
                free(c, m)
                for n, col in enumerate((col_a, col_b)):
                    sp.dma_start(slot4(c, n * FW, FW), cols_of(w, row, col, FW)).then_inc(w_in[c % RAW], 16)

            def load_rows(c, m, w, row):
                free(c, m)
                sp.dma_start(raw[:, c % RAW, :].rearrange("p (t n) -> p t n", t=2),
                             w[ds(row, 2 * P), :].rearrange("(t p) n -> p t n", p=P)).then_inc(w_in[c % RAW], 32)

            def load_ada(u, h, k=0):
                t = u if u < 3 else u + 1
                w, t0 = (ada_w[0], 0) if t < 12 else (kv_ada_w, 12) if t < 16 else (ada_w[1], 16)
                if u > 0:
                    sp.wait_ge(ada_step, 8 * (u - 1) + 4 * (h + 1) + 16 * k)
                sp.dma_start(ada[:, h, :].rearrange("p (t n) -> p t n", t=4),
                             cols_of(w, h * 4 * P, k * 2 * TW + (t - t0) * TW, TW)).then_inc(ada_in[h], 16)

            for row, src in ((0, ada_b[0]), (48, kv_ada_b), (64, ada_b[1])):
                n = src.shape[0] // P
                sp.dma_start(rows[row:row + n, 0, :], src.rearrange("(r c) -> r c", c=P)).then_inc(small_in, 16)
            load_ada(0, 0)
            load_ada(0, 1)
            sp.dma_start(x[:, :, :], x_d[0].rearrange("(b p) d -> p b d", p=P)).then_inc(x_in, 16)
            with nc.allow_non_contiguous_dma(reason="256 positions, one per partition"):
                sp.dma_start(pos_i[:, :], pos_d[0].rearrange("(b p) -> p b", p=P)).then_inc(pos_in, 16)
            sp.dma_start(freq, freq_d.to_broadcast([P, DK // 2])).then_inc(pos_in, 16)

            w_r = ret_w_in[0]
            K0, V0, G0 = RET_HEADS * DK, 2 * RET_HEADS * DK, 2 * RET_HEADS * DK + RET_HEADS * DV

            def load_decay(i):
                sp.dma_start(decay, decay_d[ds(i * P, P), :].rearrange("p (h t) -> p h t", h=2)).then_inc(decay_in, 16)

            for h in range(2):
                sp.dma_start(ada_first[:, h, :].rearrange("p (t n) -> p t n", t=4),
                             cols_of(ada_w[0], h * 4 * P, 3 * TW, TW)).then_inc(first_in, 16)
            load_ada(1, 0)
            load_ada(1, 1)
            load_half2(0, 0, w_r, 0, 0, K0)
            load_ada(2, 0)
            load_ada(2, 1)
            load_half2(1, 0, w_r, 4 * P, 0, K0)
            load_tile(2, 0, w_r, 0, V0)
            sp.wait_ge(first_done, 1)
            load_tile(4, 0, w_r, 0, G0)
            with sp.Fori(0, PAIRS - 1) as k:
                load_half2(6, k, w_r, 0, k * 2 * DK + 2 * DK, k * 2 * DK + (2 * DK + K0))
                load_ada(3, 0, k)
                load_half2(7, k, w_r, 4 * P, k * 2 * DK + 2 * DK, k * 2 * DK + (2 * DK + K0))
                load_ada(3, 1, k)
                load_half(8, k, w_r, 0, k * 2 * DV + (V0 + 2 * DV))
                sp.wait_ge(ada_step, 26 + 16 * k)
                load_decay(k)
                load_half(9, k, w_r, 4 * P, k * 2 * DV + (V0 + 2 * DV))
                load_ada(4, 0, k)
                load_half(10, k, w_r, 0, k * 2 * DV + (G0 + 2 * DV))
                load_ada(4, 1, k)
                load_half(11, k, w_r, 4 * P, k * 2 * DV + (G0 + 2 * DV))

            for m in range(8):
                load_rows(U_OUT + m, 0, ret_w_out[0], m * 2 * P)
                if m == 2:
                    sp.wait_ge(pt_ok, PAIRS - 1)
                    load_decay(PAIRS - 1)
                if m in (0, 1):
                    load_ada(9, m)
                if m in (3, 4):
                    load_ada(10, m - 3)
                if m >= 6:
                    load_ada(11, m - 6)

            def load_in(c, m, j, h):
                load_half2(c, m, ff_w_in[0], h * 4 * P, j * FW, j * FW + FF)

            c = U_FF
            load_in(c, 0, 0, 0)
            load_in(c + 1, 0, 0, 1)
            load_ada(12, 0)
            load_in(c + 2, 0, 1, 0)
            load_ada(12, 1)
            load_in(c + 3, 0, 1, 1)
            load_rows(c + 4, 0, ff_w_out[0], 0)
            load_ada(13, 0)
            load_in(c + 5, 0, 2, 0)
            load_ada(13, 1)
            load_in(c + 6, 0, 2, 1)
            load_rows(c + 7, 0, ff_w_out[0], 2 * P)
            load_in(c + 8, 0, 3, 0)
            load_ada(14, 0)
            load_in(c + 9, 0, 3, 1)
            load_ada(14, 1)
            load_rows(c + 10, 0, ff_w_out[0], 4 * P)
            with sp.Fori(0, 3) as k:
                for o in range(2):
                    load_in(c + 11 + 3 * o, k, 2 * k + (4 + o), 0)
                    load_in(c + 12 + 3 * o, k, 2 * k + (4 + o), 1)
                    load_ada(15 + o, 0, k)
                    load_rows(c + 13 + 3 * o, k, ff_w_out[0], k * 4 * P + (3 + o) * 2 * P)
                    load_ada(15 + o, 1, k)
            load_in(c + 29, 0, 10, 0)
            load_in(c + 30, 0, 10, 1)
            load_ada(21, 0)
            load_rows(c + 31, 0, ff_w_out[0], 9 * 2 * P)
            load_ada(21, 1)
            load_rows(c + 32, 0, ff_w_out[0], 10 * 2 * P)
            halves = [(kv_w, h, col) for col in (D, D + TW, 0, TW) for h in range(2)]
            halves += [(w, h, t * TW) for w in (sb_w_q[0], sb_w_out[0]) for t in range(2) for h in range(2)]
            ada_after = {0: (22, 0), 1: (22, 1), 3: (23, 0), 4: (23, 1), 6: (24, 0), 8: (24, 1), 11: (25, 0), 13: (25, 1),
                         15: (26, 0)}
            for n, (w, h, col) in enumerate(halves):
                load_half(U_KV + n, 0, w, h * 4 * P, col)
                if n in ada_after:
                    load_ada(*ada_after[n])
            load_ada(26, 1)

            w_ab = moe_w_in[0].rearrange("e k n -> (e k) n")
            w_dn = moe_w_out[0].rearrange("e k n -> (e k) n")

            def experts(m_pass):
                def load_ab(c, m, e, col):
                    for ab in range(2):
                        load_tile(c + 2 * ab, m, w_ab, e * D, col + ab * FE)

                def load_out(c, m, e, row):
                    for h in range(2):
                        load_rows(c + h, m, w_dn, e * FE + (row + h * 2 * P))

                def later_tiles(e, m):
                    with sp.Fori(0, ET - 1) as k:
                        load_ab(U_MOE + 4, m + k, e, k * TW + TW)
                        load_out(U_MOE + 8, m + k, e, k * TW)

                load_ab(U_MOE, m_pass, 0, 0)
                with sp.Fori(0, NE - 1) as e:
                    m = ET * e + m_pass
                    later_tiles(e, m)
                    load_ab(U_MOE + MOE_U - 2, m, e + 1, 0)
                    load_out(U_MOE + MOE_U + 2, m, e, (ET - 1) * TW)
                m = m_pass + ET * (NE - 1)
                later_tiles(NE - 1, m)
                load_out(U_MOE + MOE_U - 2, m, NE - 1, (ET - 1) * TW)

            experts(0)
            sp.wait_ge(npass_ok, 1)
            npass = sp.value_load(npass_t[0:1, 0:1], min_val=1, max_val=2)
            with sp.If(npass - 1):
                experts(NE * ET)
            sp.dma_start(fnorm, final_norm.rearrange("(a d) -> a d", a=1).to_broadcast([P, D])).then_inc(fnorm_in, 16)
            for b in range(NB):
                sp.wait_ge(o_ok, b + 1)
                sp.dma_start(out_d[0, b * P:(b + 1) * P, :], x[:, b, :]).then_inc(stored, 16)
            sp.wait_ge(stored, NB * 16)

        @block.gpsimd
        def _(pool):
            steps = Chain(pool, pchain)
            steps.link(pool.memset(ones[:, :], 1.0))
            pool.memset(eps[:, :], EPS)
            steps.link(pool.iota(slot_no[:, :], pattern=[[1, P]], base=0, channel_multiplier=0,
                                 allow_small_or_imprecise_dtypes=True))
            pool.affine_select(out=ident[:, :], in_=ones[:, :], compare_op=ALU.is_equal, fill=0.0, base=0,
                               pattern=[[-1, P]], channel_multiplier=1)
            pool.affine_select(out=before[:, :], in_=ones[:, :], compare_op=ALU.is_gt, fill=0.0, base=0,
                               pattern=[[1, P]], channel_multiplier=-1)
            pool.affine_select(out=after[:, :], in_=ones[:, :], compare_op=ALU.is_gt, fill=0.0, base=0,
                               pattern=[[-1, P]], channel_multiplier=1)
            pool.affine_select(out=causal[:, :], in_=ones[:, :], compare_op=ALU.is_gt, fill=0.0, base=0,
                               pattern=[[1, P]], channel_multiplier=-1).then_inc(const_ok, 1)

            def diagonal(g, dg, col, tiles):
                pool.wait_ge(mod_ok, tiles)
                pool.tensor_tensor(dg, ident[:, :].unsqueeze(1).to_broadcast([P, KC, P]),
                                   modc[:, col:col + KC].unsqueeze(2).to_broadcast([P, KC, P]),
                                   ALU.mult).then_inc(diag_ok, 1)

            def rope(i):
                cs, sn = (t[:, :, :].unsqueeze(2).to_broadcast([P, NB, 4, DK // 2]) for t in (cos, sin))
                src = qk.rearrange("p b (g r f) -> p b g r f", g=4, r=2)
                dst = qkr.rearrange("p b (g r f) -> p b g r f", g=4, r=2)
                t1, t2, o1, o2 = src[:, :, :, 0, :], src[:, :, :, 1, :], dst[:, :, :, 0, :], dst[:, :, :, 1, :]
                ta, tb = (rope_t[:, n, :].rearrange("p (b g f) -> p b g f", b=NB, g=4) for n in range(2))
                pool.wait_ge(qk_ev, i + 1)
                pool.tensor_tensor(ta, t1, cs, ALU.mult)
                steps.link(pool.tensor_tensor(tb, t2, sn, ALU.mult))
                if not isinstance(i, int):
                    pool.wait_ge(qkT_done, i)
                steps.link(pool.tensor_tensor(o1, ta, tb, ALU.subtract))
                pool.tensor_tensor(ta, t1, sn, ALU.mult)
                steps.link(pool.tensor_tensor(tb, t2, cs, ALU.mult))
                pool.tensor_tensor(o2, ta, tb, ALU.add).then_inc(roped, 1)

            pool.wait_ge(rt_ok, 2)
            rope(0)
            with pool.Fori(0, PAIRS - 1) as k:
                steps.enter(k, 3)
                rope(k + 1)
                steps.leave(PAIRS - 1)

            pool.wait_ge(qkT_done, PAIRS)
            diagonal(0, diag0, MIX0 + G, 5)
            diagonal(1, diag1, FF0 + G, 11)

            mask = causal[:, :].unsqueeze(1).unsqueeze(1).to_broadcast([P, 2, 2, P])
            pool.wait_ge(ada_step, 27 * 8)
            diagonal(2, diag2, MIX1 + G, 21)
            for c in range(KC):
                pool.wait_ge(a0_ok, c + 1)
                a = on_diagonal(at_buf(c, 0))
                pool.tensor_tensor(a, a, mask, ALU.mult).then_inc(am_ok, 1)
            pool.wait_ge(gbc_done, 3)
            diagonal(3, diag3, FF1 + G, 27)

        @block.tensor
        def _(pe):
            def passes(out, a_hi, a_lo, b_hi, b_lo, first, last):
                pe.matmul(out, a_hi, b_hi, start=first, stop=False)
                pe.matmul(out, a_hi, b_lo, start=False, stop=False)
                return pe.matmul(out, a_lo, b_hi, start=False, stop=last)

            def landed(c, m, q):
                pe.wait_ge(lo_done, before_half(c, m) + (q + 1))

            def by_rows(c, m, a_hi, a_lo, kc0, blocks, bank0, first, last_one):
                s = c % RING
                for t in range(2):
                    landed(c, m, t)
                    for b in range(blocks):
                        tok = slice(b * P, (b + 1) * P)
                        for n in range(2):
                            cols = slice(t * D + n * TW, t * D + (n + 1) * TW)
                            last = passes(ps[:, bank0 + 2 * b + n, :], a_hi[:, kc0 + t, tok], a_lo[:, kc0 + t, tok],
                                          w_hi[:, s, cols], w_lo[:, s, cols], first and t == 0, last_one and t == 1)
                    last.then_inc(w_used, 1)

            def reduce_ada(u, bank, k=0):
                pe.wait_ge(ada_step, 8 * (u + 1) + 16 * k)
                for c in range(4):
                    last = pe.transpose(ps[:, bank, c * P:(c + 1) * P], acc[:, u % 2, c * P:(c + 1) * P], ident[:, :])
                last.then_inc(acc_red, 1)

            def transpose_x(n):
                for b in range(NB):
                    pe.wait_ge(xn_ok, 2 * n + b + 1)
                    for c in range(KC):
                        last = pe.transpose(ps[:, c // 2, (c % 2) * S + b * P:(c % 2) * S + (b + 1) * P],
                                            (xn0 if n == 0 else xn)[:, b, c * P:(c + 1) * P], ident[:, :])
                        if b == NB - 1 and c % 2:
                            last.then_inc(xT_done, 1)

            def broadcast_gate(g, dg, bank):
                pe.wait_ge(diag_ok, g + 1)
                for n in range(2):
                    last = pe.matmul(ps[:, bank + n, :], ones[:, :],
                                     dg[:, 4 * n:4 * n + 4, :].rearrange("p c q -> p (c q)"), start=True, stop=True)
                last.then_inc(gbc_done, 1)

            pe.wait_ge(const_ok, 1)
            pe.wait_ge(small_in, 8 * 16)
            pe.transpose(ps[:, 4, 0:P], rows[:, 0, :], ident[:, :])
            pe.transpose(ps[:, 4, P:P + 48], rows[0:48, 1, :], ident[0:48, 0:48]).then_inc(vecT_done, 1)
            reduce_ada(0, 6)
            transpose_x(0)
            pe.wait_ge(cond_ok, 1)
            pe.wait_ge(first_in, 32)
            for c in range(4):
                for kc in range(KC):
                    cols = slice(kc % 4 * TW + c * P, kc % 4 * TW + (c + 1) * P)
                    last = pe.matmul(ps[:, 5, c:c + 1], ada_first[:, kc // 4, cols], cond[:, kc:kc + 1],
                                     start=kc == 0, stop=kc == KC - 1)
            last.then_inc(first_done, 1)
            reduce_ada(1, 7)
            pe.wait_ge(mod_ok, 1)
            reduce_ada(2, 6)

            def transpose_r(i):
                pe.wait_ge(r_ok, i + 1)
                for c in range(4):
                    for b in range(NB):
                        last = pe.transpose(ps[:, 6 + c // 2, (c % 2) * S + b * P:(c % 2) * S + (b + 1) * P],
                                            gs[:, b, c * P:(c + 1) * P], ident[:, :])
                last.then_inc(outT_done, 1)

            def tile(c, m, banks, q=None, a_hi=hT_hi, a_lo=hT_lo):
                for h in range(2):
                    s = (c + h) % RING
                    for t in range(4):
                        if t % 2 == 0:
                            if q is not None:
                                pe.wait_ge(h_ok, 4 * q + 2 * h + t // 2 + 1)
                            landed(c + h, m, t // 2)
                        kc = 4 * h + t
                        cols = slice(t * TW, (t + 1) * TW)
                        for b, bank in enumerate(banks):
                            tok = slice(b * P, (b + 1) * P)
                            last = passes(ps[:, bank, :], a_hi[:, kc, tok], a_lo[:, kc, tok],
                                          w_hi[:, s, cols], w_lo[:, s, cols], kc == 0, kc == KC - 1)
                        if t % 2:
                            last.then_inc(w_used, 1)

            def mix(i):
                pe.wait_ge(pt_ok, i + 1)
                pe.wait_ge(v_ev, i + 1)
                for hd in range(2):
                    vc = slice(hd * DV, (hd + 1) * DV)
                    pe.matmul(ps[:, 4, vc], PT[:, hd, 0:P], v_t[:, 0, vc], start=True, stop=True)
                    pe.matmul(ps[:, 5, vc], PT[:, hd, P:S], v_t[:, 0, vc], start=True, stop=False)
                    last = pe.matmul(ps[:, 5, vc], PT[:, hd, S:384], v_t[:, 1, vc], start=False, stop=True)
                last.then_inc(pv_done, 1)

            def pair_of_heads(i, m):
                later = not isinstance(i, int)
                if later:
                    pe.wait_ge(qk_ev, i)
                    pe.wait_ge(mod_ok, 2 * i + 1)
                tile(0, m, (0, 1), None if later else 0)
                if later:
                    pe.wait_ge(mod_ok, 2 * i + 2)
                    mix(i - 1)
                    pe.wait_ge(qk_ev, i + 1)
                    reduce_ada(4, 0, m - 1)
                    pe.wait_ge(gs_ok, i)
                tile(2, m, (2, 3))
                if later:
                    transpose_r(i - 1)
                pe.wait_ge(roped, i + 1)
                for g in range(4):
                    for b in range(NB):
                        last = pe.transpose(ps[:, 4 + g // 2, (g % 2) * S + b * P:(g % 2) * S + (b + 1) * P],
                                            qkr[:, b, g * P:(g + 1) * P], ident[:, :])
                last.then_inc(qkT_done, 1)
                pe.wait_ge(v_ev, i + 1)
                tile(4, m, (2, 3))
                pe.wait_ge(qkT_ev, i + 1)
                reduce_ada(3, 4, m)
                if later:
                    pe.wait_ge(r32_ok, i)
                else:
                    pe.wait_ge(mod_ok, 3)
                for hd in range(2):
                    pe.matmul(ps[:, 6 + hd, 0:S], qkT[:, 2 + hd, 0:P], qkT[:, hd, :], start=True, stop=True)
                    last = pe.matmul(ps[:, 6 + hd, S:384], qkT[:, 2 + hd, P:S], qkT[:, hd, P:S], start=True, stop=True)
                last.then_inc(sc_done, 1)

            pair_of_heads(0, 0)
            with pe.Fori(0, PAIRS - 1) as k:
                pair_of_heads(k + 1, k + 1)

            pe.wait_ge(gs_ok, PAIRS)
            pe.wait_ge(v_ev, PAIRS)
            for m in range(8):
                if m == 4:
                    pe.wait_ge(rTl_ok, PAIRS - 1)
                if m == 6:
                    pe.wait_ge(rTl_ok, PAIRS)
                by_rows(U_OUT + m, 0, rT_hi, rT_lo, 2 * m, NB, 0, m == 0, m == 7)
                if m == 1:
                    pe.wait_ge(mod_ok, 2 * PAIRS + 2)
                    mix(PAIRS - 1)
                    reduce_ada(10, 6)
                if m == 3:
                    pe.wait_ge(mod_ok, 11)
                    transpose_r(PAIRS - 1)
                    broadcast_gate(0, diag0, 4)
                if m == 4:
                    pe.wait_ge(r32_ok, PAIRS)
                    broadcast_gate(1, diag1, 6)
                if m == 5:
                    pe.wait_ge(gbc_ev, 1)
                    reduce_ada(11, 4)
                if m == 6:
                    reduce_ada(12, 5)

            pe.wait_ge(x_ok, 2)
            transpose_x(1)

            def ff_in(c, m, j):
                if isinstance(j, int) and j == 0:
                    tile(c, m, (0, 1), 1)
                else:
                    pe.wait_ge(fg_ok, j)
                    tile(c, m, (0, 1))

            def ff_T(j):
                pe.wait_ge(fg_ok, j + 1)
                if not (isinstance(j, int) and j == 0):
                    pe.wait_ge(fTl_ok, j)
                for c in range(2):
                    for b in range(NB):
                        last = pe.transpose(ps[:, 2, c * S + b * P:c * S + (b + 1) * P],
                                            f_g[:, b, c * P:(c + 1) * P], ident[:, :])
                last.then_inc(fT_done, 1)

            def ff_out(c, m, j, first, last_one):
                pe.wait_ge(fTl_ok, j + 1)
                by_rows(c, m, fT_hi, fT_lo, 0, NB, 4, first, last_one)

            ff_in(U_FF, 0, 0)
            pe.wait_ge(h_ok, 8)
            ff_T(0)

            def ff_two(i, m):
                for o in range(2):
                    c = U_FF + 2 + 3 * o
                    ff_in(c, m, 2 * i + (1 + o))
                    pe.wait_ge(mod_ok, 2 * i + (13 + o))
                    reduce_ada(13 + o, 3, i)
                    ff_out(c + 2, m, 2 * i + o, isinstance(i, int) and o == 0, False)
                    ff_T(2 * i + (1 + o))

            ff_two(0, 0)
            with pe.Fori(0, 4) as k:
                ff_two(k + 1, k + 1)
            ff_out(U_FF + 32, 0, FT - 1, False, True)
            pe.wait_ge(mod_ok, 23)
            reduce_ada(23, 3)

            pe.wait_ge(mod_ok, 24)
            transpose_x(2)

            def transpose_kq(n):
                pe.wait_ge(kv_ev, n + 3)
                bank = 2 * (n % 2)
                for c in range(4):
                    for b in range(NB):
                        last = pe.transpose(ps[:, bank + c // 2, (c % 2) * S + b * P:(c % 2) * S + (b + 1) * P],
                                            qk_t[n % 2][:, b, c * P:(c + 1) * P], ident[:, :])
                last.then_inc(kqT_done, 1)

            pe.wait_ge(x_ok, 4)
            tile(U_KV, 0, (4, 5), 2)
            tile(U_KV + 2, 0, (6, 7))
            pe.wait_ge(kv_ev, 1)
            tile(U_KV + 4, 0, (4, 5))
            pe.wait_ge(kv_ev, 2)
            tile(U_KV + 6, 0, (6, 7))
            pe.wait_ge(h_ok, 16)
            reduce_ada(24, 2)
            transpose_kq(0)
            tile(U_Q, 0, (4, 5), 3, hq_hi, hq_lo)
            pe.wait_ge(mod_ok, 25)
            transpose_kq(1)
            tile(U_Q + 2, 0, (6, 7), 3, hq_hi, hq_lo)
            pe.wait_ge(kqT_ev, 1)
            transpose_kq(2)
            pe.wait_ge(kqT_ev, 2)
            transpose_kq(3)
            reduce_ada(25, 4)
            reduce_ada(26, 5)

            def scores(c):
                if c < 2:
                    pe.wait_ge(kqT_ev, c + 3)
                elif c == 2:
                    pe.wait_ge(mod_ok, 27)
                else:
                    pe.wait_ge(u_ok, c - 2)
                for h in range(2):
                    r = slice(DH * h, DH * (h + 1))
                    o = ps[:, 2 * (c % 3) + h, :]
                    pe.matmul(o[:, 0:S], kT[r, c, 0:P], qT[r, c, :], start=True, stop=True)
                    last = pe.matmul(o[:, S:384], kT[r, c, P:S], qT[r, c, P:S], start=True, stop=True)
                last.then_inc(z_done, 1)

            def tails(c):
                pe.wait_ge(lm_ok, c + 1)
                lm = at_buf(c, 1)
                for h in range(2):
                    o = ps[:, 2 * (c % 3) + h, :]
                    pe.matmul(o[:, 0:S], after[:, :], lm[:, h, 0:S], start=True, stop=False)
                    pe.matmul(o[:, P:S], ones[:, :], lm[:, h, S:384], start=False, stop=True)
                    last = pe.matmul(o[:, S:384], after[:, :], lm[:, h, S:384], start=True, stop=True)
                last.then_inc(tail_done, 1)

            def mix_values(c):
                pe.wait_ge(am_ok, c + 1)
                if c >= 2:
                    pe.wait_ge(ol_ok, c - 1)
                a = at_buf(c, 0)
                for h in range(2):
                    o = ps[DH * h:DH * (h + 1), 6 + c % 2, :]
                    vc = slice((2 * c + h) * DH, (2 * c + h + 1) * DH)
                    pe.matmul(o[:, 0:S], v_all[:, 0, vc], a[:, h, 0:S], start=True, stop=False)
                    last = pe.matmul(o[:, P:S], v_all[:, 1, vc], a[:, h, S:384], start=False, stop=True)
                last.then_inc(av_done, 1)

            scores(0)
            scores(1)
            for g in range(KC // 2):
                c = 2 * g
                if c + 2 < KC:
                    scores(c + 2)
                if g:
                    mix_values(c - 2)
                    mix_values(c - 1)
                tails(c)
                tails(c + 1)
                if c + 3 < KC:
                    scores(c + 3)
            mix_values(KC - 2)
            mix_values(KC - 1)
            broadcast_gate(2, diag2, 4)
            pe.wait_ge(u_ok, KC)

            pe.wait_ge(ol_ok, KC)
            for t in range(2):
                for h in range(2):
                    c = U_SBO + 2 * t + h
                    for q in range(4):
                        if q % 2 == 0:
                            landed(c, 0, q // 2)
                        kc, cols = 4 * h + q, slice(q * TW, (q + 1) * TW)
                        for b in range(NB):
                            tok = slice(b * P, (b + 1) * P)
                            last = passes(ps[:, 2 * b + t, :], oT_hi[:, kc, tok], oT_lo[:, kc, tok],
                                          w_hi[:, c % RING, cols], w_lo[:, c % RING, cols], kc == 0, kc == KC - 1)
                        if q % 2:
                            last.then_inc(w_used, 1)

            broadcast_gate(3, diag3, 6)
            pe.wait_ge(x_ok, 6)
            transpose_x(3)
            pe.wait_ge(h32a_ok, 10)
            pe.wait_ge(h32b_ok, 10)
            for b in range(NB):
                for c in range(KC):
                    last = pe.transpose(ps[:, 2 * b + c // 4, (c % 4) * P:(c % 4 + 1) * P],
                                        h32[:, c, b * P:(b + 1) * P], ident[:, :])
            last.then_inc(hk_done, 1)
            pe.wait_ge(rw_in, 16)
            for b in range(NB):
                for kc in range(KC):
                    last = pe.matmul(ps[:, 4, b * NE:(b + 1) * NE], h32[:, kc, b * P:(b + 1) * P], rw[:, kc, :],
                                     start=kc == 0, stop=kc == KC - 1)
            last.then_inc(rt_done, 1)
            pe.wait_ge(sel_ok, 1)
            pe.matmul(ps[:, 5, 0:8], before[:, :], sel[:, 0, :], start=True, stop=True)
            pe.matmul(ps[:, 5, 8:16], ones[:, :], sel[:, 0, :], start=True, stop=False)
            pe.matmul(ps[:, 5, 8:16], before[:, :], sel[:, 1, :], start=False, stop=True)
            pe.matmul(ps[:, 5, 16:24], ones[:, :], sel[:, 0, :], start=True, stop=False)
            pe.matmul(ps[:, 5, 16:24], ones[:, :], sel[:, 1, :], start=False, stop=True).then_inc(cnt_done, 1)

            def up(c, m, bank):
                for h in range(2):
                    s = (c + h) % RING
                    for t in range(4):
                        if t % 2 == 0:
                            landed(c + h, m, t // 2)
                        kc, cols = 4 * h + t, slice(t * TW, (t + 1) * TW)
                        last = passes(ps[:, bank, :], hg_hi[:, kc, :], hg_lo[:, kc, :], w_hi[:, s, cols],
                                      w_lo[:, s, cols], kc == 0, kc == KC - 1)
                        if t % 2:
                            last.then_inc(w_used, 1)

            def down(c, m, n, first, last_one):
                pe.wait_ge(eTl_ok, n + 1)
                for h in range(2):
                    by_rows(c + h, m, eT_hi, eT_lo, 2 * h, 1, 4, first and h == 0, last_one and h == 1)

            def transpose_product(n):
                pe.wait_ge(eg_ok, n + 1)
                for c in range(4):
                    last = pe.transpose(ps[:, 2, c * P:(c + 1) * P], e_g[:, c * P:(c + 1) * P], ident[:, :])
                last.then_inc(eT_done, 1)

            def gather(ne):
                pe.wait_ge(hot_ok, ne + 1)
                for n in range(2):
                    cols = slice(n * TW, (n + 1) * TW)
                    for b in range(NB):
                        pe.matmul(ps[:, 6 + n, :], hot[:, b, :], hk_hi[:, b, cols], start=b == 0, stop=False)
                        last = pe.matmul(ps[:, 6 + n, :], hot[:, b, :], hk_lo[:, b, cols], start=False,
                                         stop=b == NB - 1)
                last.then_inc(ga_done, 1)

            def transpose_gathered(ne):
                pe.wait_ge(ht_ok, ne + 1)
                for c in range(KC):
                    last = pe.transpose(ps[:, 6 + c // 4, (c % 4) * P:(c % 4 + 1) * P], ht[:, c * P:(c + 1) * P],
                                        ident[:, :])
                last.then_inc(hgT_done, 1)

            def transpose_hot():
                for b in range(NB):
                    last = pe.transpose(ps[:, 3, b * P:(b + 1) * P], hot[:, b, :].bitcast(f32), ident[:, :])
                last.then_inc(hotT_done, 1)

            def scatter(ne):
                pe.wait_ge(yl_ok, ne + 1)
                pe.wait_ge(hotT_ok, ne + 1)
                for b in range(NB):
                    for n in range(2):
                        o, cols = ps[:, 6 - 2 * b + n, :], slice(n * TW, (n + 1) * TW)
                        pe.matmul(o, hotT[:, b * P:(b + 1) * P], y_hi[:, cols], start=True, stop=False)
                        last = pe.matmul(o, hotT[:, b * P:(b + 1) * P], y_lo[:, cols], start=False, stop=True)
                    last.then_inc(scat_done, 1)

            def step(j, me, ne, more=True):
                c, n = U_MOE + 4 + RAW * (j - 1), me + j
                pe.wait_ge(eg_ok, n)
                up(c, me, 0)
                if j == ET + 1:
                    scatter(ne)
                up(c + 2, me, 1)
                if j == 2:
                    transpose_hot()
                if j == ET - 1 and more:
                    transpose_gathered(ne + 1)
                if j == ET + 1:
                    pe.wait_ge(yacc_ok, NB * (ne + 1))
                down(c + 4, me, n - 1, j == 1 or j == ET + 1, j == ET)
                if j == ET - 2 and more:
                    gather(ne + 1)
                transpose_product(n)

            pe.wait_ge(hk_ok, 1)
            gather(0)
            pe.wait_ge(npass_ok, 1)
            npass = pe.value_load(npass_t[0:1, 0:1], min_val=1, max_val=2)
            with pe.Fori(0, npass) as p:
                m0 = NE * ET * p
                with pe.If(p):
                    gather(NE * p)
                transpose_gathered(NE * p)
                pe.wait_ge(hgl_ok, NE * p + 1)
                up(U_MOE, m0, 0)
                up(U_MOE + 2, m0, 1)
                transpose_product(m0)
                step(1, m0, NE * p)
                with pe.Fori(0, NE - 1) as e:
                    ne = NE * p + e
                    me = ET * ne
                    for j in range(2, ET + 2):
                        if j == ET:
                            pe.wait_ge(hgl_ok, ne + 2)
                        step(j, me, ne)
                ne = NE * p + (NE - 1)
                me = ET * ne
                for j in range(2, ET):
                    step(j, me, ne, more=False)
                down(U_MOE + MOE_U - 2, me, me + (ET - 1), False, True)
                scatter(ne)

        @block.scalar
        def _(act):
            steps = Chain(act, achain)

            def split_quarters(c, m, first, end):
                for n in range(first, end):
                    cn, cols = c + n // 2, slice(n % 2 * HALF // 2, (n % 2 + 1) * HALF // 2)
                    if n == first or n % 2 == 0:
                        act.wait_ge(w_in[cn % RAW], 32 * (cn // RAW + 1) + 32 * m)
                    if cn >= RING:
                        act.wait_ge(w_used, before_half(cn - RING, m) + (n % 2 + 1))
                    act.activation(w_hi[:, cn % RING, cols], raw[:, cn % RAW, cols], ACT.Copy).then_inc(hi_done, 1)

            def split(c, m=0):
                split_quarters(c, m, 0, 2)

            def root_mean_square(n):
                act.activation(stat[:, 18:19], eps[:, :], ACT.Sqrt)
                for b in range(NB):
                    if 0 < n < 4:
                        act.wait_ge(x_ok, NB * (n - 1) + b + 1)
                    if n == 4 and b == 0:
                        act.wait_ge(yacc_ok, NB * NE * npass)
                    act.activation((xn0 if n == 0 else xn)[:, b, :], x[:, b, :], ACT.Square,
                                   accum_out=stat[:, b:b + 1]).then_inc(ss_ok, 1)
                act.wait_ge(ss_ok, NB * (n + 1))
                act.activation(stat[:, 4:6], stat[:, 0:2], ACT.Sqrt, bias=eps[:, :], scale=1.0 / D).then_inc(rs_ok, 1)

            def head_roots(i):
                act.wait_ge(var_ok, i + 1)
                act.activation(stat[:, 24:28], mv[:, :, 1], ACT.Sqrt, bias=eps[:, :]).then_inc(sd_ok, 1)

            def modulate(q, n, shift, hT_free, dst=hT_hi):
                def bank(i):
                    act.wait_ge(xT_done, 4 * n + i + 1)
                    if i == 0:
                        act.wait_ge(scol_ok, q + 1)
                    if q == 3:
                        act.wait_ge(h_ok, 4 * 2 + i + 1)
                    for c in (2 * i, 2 * i + 1):
                        ins = act.activation(h32_at(q)[:, c, :], ps[:, i, (c % 2) * S:(c % 2 + 1) * S], ACT.Identity,
                                             bias=modc[:, shift + c:shift + c + 1], scale=scol[:, q, c:c + 1])
                    ins.then_inc(h32a_ok, 1)

                def high(i):
                    act.wait_ge(h32b_ok if i % 2 else h32a_ok, 2 * q + i // 2 + 1)
                    if hT_free and i == 0:
                        act.wait_ge(w_used, before_half(hT_free))
                    act.activation(dst[:, 2 * i:2 * i + 2, :], h32_at(q)[:, 2 * i:2 * i + 2, :], ACT.Copy)\
                       .then_inc(h_hi_ok, 1)

                bank(0)
                if dst is not None:
                    high(0)
                    high(1)
                bank(2)
                if dst is not None:
                    high(2)
                    high(3)

            def gate_out(g, tile, bank):
                act.wait_ge(gbc_done, g + 1)
                act.activation(tile[:, :].rearrange("p (n q) -> p n q", n=2), ps[:, bank:bank + 2, :],
                               ACT.Copy).then_inc(gbc_ev, 1)

            for row, g, src in ((112, 0, norm_mix.rearrange("l (r c) -> (l r) c", c=P)),
                                (0, 1, norm_ff.rearrange("l (r c) -> (l r) c", c=P)),
                                (16, 1, kv_norm.rearrange("(r c) -> r c", c=P)),
                                (24, 1, ret_gn[0].rearrange("(r c) -> r c", c=P)),
                                (40, 1, c_d[0].rearrange("(r c) -> r c", c=P))):
                act.dma_start(rows[row:row + src.shape[0], g, :], src).then_inc(small_in, 16)
            act.wait_ge(vec_ok, 1)
            act.activation(cond[:, :], vec[:, V_C:V_C + KC], ACT.Silu).then_inc(cond_ok, 1)
            act.wait_ge(x_in, 16)
            root_mean_square(0)
            act.wait_ge(ang_ok, 1)
            act.activation(sin[:, :, :], red, ACT.Sin).then_inc(rt_ok, 1)
            act.activation(cos[:, :, :], tmp_r, ACT.Sin).then_inc(rt_ok, 1)
            split(0)
            split(1)
            split(2)
            modulate(0, 0, MIX0 + SH, 0)

            def high_r(i):
                act.wait_ge(r32_ok, i + 1)
                act.activation(rT_hi[:, ds(i * 4, 4), :], r32, ACT.Copy).then_inc(rTh_ok, 1)

            def pair_of_heads(i, m):
                later = not isinstance(i, int)
                if later:
                    split(2, m)
                split(3, m)
                if later:
                    act.wait_ge(roped, i)
                act.wait_ge(w_used, before_half(2, m))
                act.activation(qk, ps[:, 0:2, :], ACT.Copy).then_inc(qk_ev, 1)
                split(4, m)
                if later:
                    head_roots(i - 1)
                split(5, m)
                if later:
                    act.wait_ge(pv_done, i)
                act.wait_ge(w_used, before_half(4, m))
                act.activation(v_t, ps[:, 2:4, :], ACT.Copy).then_inc(v_ev, 1)
                split(6, m)
                if later:
                    high_r(i - 1)
                act.wait_ge(qkT_done, i + 1)
                if later:
                    act.wait_ge(sc_done, i)
                act.activation(qkT.rearrange("p (n c) s -> p n (c s)", n=2), ps[:, 4:6, :], ACT.Copy)\
                   .then_inc(qkT_ev, 1)
                split(7, m)
                if later:
                    act.wait_ge(outT_done, i)
                act.wait_ge(w_used, before_half(6, m))
                act.activation(gs, ps[:, 2:4, :], ACT.Silu).then_inc(gs_ok, 1)

            pair_of_heads(0, 0)
            with act.Fori(0, PAIRS - 1) as k:
                pair_of_heads(k + 1, k + 1)

            split(26)
            split(27)
            head_roots(PAIRS - 1)
            split(28)
            split(29)
            high_r(PAIRS - 1)
            gate_out(0, gate_m, 4)
            split(30)
            split(31)
            gate_out(1, gate_f, 6)
            split(32)
            split(33)
            split_quarters(U_FF + 2, 0, 0, 2)
            root_mean_square(1)
            modulate(1, 1, FF0 + SH, U_OUT)

            def ff_act(j, c, m):
                act.wait_ge(w_used, before_half(c, m))
                if not (isinstance(j, int) and j == 0):
                    act.wait_ge(fg_ok, j)
                act.activation(f_sa, ps[:, 0:2, 0:FW], ACT.Silu).then_inc(fsa_ok, 1)

            def ff_high(j):
                act.wait_ge(fT_done, j + 1)
                act.activation(fT_hi.rearrange("p c s -> p (c s)"), ps[:, 2, :], ACT.Copy).then_inc(fTh_ok, 1)

            split_quarters(U_FF + 2, 0, 2, 4)
            ff_act(0, U_FF + 2, 0)
            ff_high(0)
            split_quarters(U_FF + 2, 0, 4, 5)

            with act.Fori(0, 5) as k:
                for o in range(2):
                    c, j = U_FF + 2 + 3 * o, 2 * k + (1 + o)
                    split_quarters(c, k, 5, 8)
                    ff_act(j, c + 2, k)
                    split_quarters(c, k, 8, 11)
                    ff_high(j)
            split_quarters(U_KV + 1, 0, 1, 4)

            root_mean_square(2)
            modulate(2, 2, KVM + SH, U_KV - 2)
            modulate(3, 2, MIX1 + SH, 0, hq_hi)

            def tile_out(n, dst):
                act.wait_ge(w_used, before_half(U_KV + 2 * n + 2))
                bank = 4 + 2 * (n % 2)
                act.activation(dst, ps[:, bank:bank + 2, :], ACT.Copy).then_inc(kv_ev, 1)

            def kq_out(n):
                act.wait_ge(kqT_done, n + 1)
                bank = 2 * (n % 2)
                dst = (kT if n < 2 else qT)[:, 4 * (n % 2):4 * (n % 2) + 4, :]
                act.activation(dst.rearrange("p (n c) s -> p n (c s)", n=2), ps[:, bank:bank + 2, :], ACT.Copy,
                               scale=1.0 if n < 2 else DH ** -0.5).then_inc(kqT_ev, 1)

            split_quarters(U_KV, 0, 6, 9)
            tile_out(0, v_all[:, :, 0:TW])
            split_quarters(U_KV, 0, 9, 13)
            tile_out(1, v_all[:, :, TW:D])
            split_quarters(U_KV, 0, 13, 17)
            tile_out(2, qk_t[0])
            split_quarters(U_KV, 0, 17, 21)
            act.wait_ge(h_ok, 16)
            tile_out(3, qk_t[1])
            kq_out(0)
            split_quarters(U_KV, 0, 21, 25)
            tile_out(4, qk_t[0])
            kq_out(1)
            split_quarters(U_KV, 0, 25, 29)
            act.wait_ge(kqT_done, 2)
            tile_out(5, qk_t[1])
            kq_out(2)
            kq_out(3)
            split_quarters(U_KV, 0, 29, 30)

            def decline(c):
                act.wait_ge(z_done, c + 1)
                if c == 1:
                    act.wait_ge(ada_step, 27 * 8)
                if c >= 4:
                    act.wait_ge(av_done, c - 3)
                b0 = at_buf(c, 0)
                steps.link(act.activation(b0, ps[:, 2 * (c % 3):2 * (c % 3) + 2, 0:384], ACT.Abs))
                act.activation(b0, b0, ACT.Exp, scale=-1.0).then_inc(e_ok, 1)

            def logarithm(c):
                act.wait_ge(e_ok, c + 1)
                act.activation(at_buf(c, 0), at_buf(c, 0), ACT.Ln, bias=ones[:, 0:1]).then_inc(sm_ok, 1)

            def weights(c):
                act.wait_ge(u_ok, c + 1)
                act.activation(at_buf(c, 0), at_buf(c, 0), ACT.Exp).then_inc(a0_ok, 1)

            def high_o(c):
                act.wait_ge(av_done, c + 1)
                act.activation(oT_hi[:, c, :], ps[:, 6 + c % 2, 0:S], ACT.Copy).then_inc(oh_ok, 1)

            for c in range(0, KC, 2):
                for h in range(2):
                    decline(c + h)
                    if c:
                        weights(c - 2 + h)
                logarithm(c)
                logarithm(c + 1)
                if c:
                    high_o(c - 2)
                    high_o(c - 1)
            act.dma_start(rw, router[0].rearrange("(t p) e -> p t e", p=P)).then_inc(rw_in, 16)
            weights(KC - 2)
            weights(KC - 1)
            high_o(KC - 2)
            high_o(KC - 1)
            gate_out(2, gate_m, 4)
            split_quarters(U_KV, 0, 30, 32)

            gate_out(3, gate_f, 6)
            root_mean_square(3)
            split(U_MOE)
            modulate(4, 3, FF1 + SH, 0, None)
            split(U_MOE + 1)
            act.wait_ge(hk_done, 1)
            act.activation(hk_hi.rearrange("p b (n q) -> p (b n) q", n=2), ps[:, 0:4, :], ACT.Copy)\
               .then_inc(hk_hi_ok, 1)
            split(U_MOE + 2)
            act.wait_ge(dm_ok, 1)
            act.activation(stat[:, 34:36], stat[:, 32:34], ACT.Exp).then_inc(ex_ok, 1)

            def tile_silu(n, c, m):
                act.wait_ge(w_used, before_half(c, m))
                act.activation(e_sa, ps[:, 0, :], ACT.Silu).then_inc(esa_ok, 1)

            def tile_high(n):
                act.wait_ge(eT_done, n + 1)
                act.activation(eT_hi.rearrange("p c s -> p (c s)"), ps[:, 2, :], ACT.Copy).then_inc(eTh_ok, 1)

            def gathered_out(ne):
                act.wait_ge(ga_done, ne + 1)
                act.activation(ht.rearrange("p (n q) -> p n q", n=2), ps[:, 6:8, :], ACT.Copy).then_inc(ht_ok, 1)

            def gathered_high(ne):
                act.wait_ge(hgT_done, ne + 1)
                act.activation(hg_hi.rearrange("p (n c) s -> p n (c s)", n=2), ps[:, 6:8, :], ACT.Copy)\
                   .then_inc(hgh_ok, 1)

            def y_high(ne):
                act.wait_ge(yg_ok, ne + 1)
                act.activation(y_hi, y32, ACT.Copy).then_inc(yh_ok, 1)

            def step(j, me, ne, more=True):
                c, n = U_MOE + 4 + RAW * (j - 1), me + j
                split_quarters(c, me, 5, 9)
                act.wait_ge(eg_ok, n)
                tile_silu(n, c + 2, me)
                split_quarters(c, me, 9, 12)
                if j < ET - 1 or more:
                    split_quarters(c, me, 12, 14)
                    if j == ET - 1:
                        gathered_high(ne + 1)
                    split_quarters(c, me, 14, 17)
                tile_high(n)
                if j == ET:
                    y_high(ne)
                if j == 2:
                    act.wait_ge(hotT_done, ne + 1)
                    act.activation(hotT, ps[:, 3, 0:S], ACT.Copy).then_inc(hotT_ok, 1)
                if j == ET - 2 and more:
                    gathered_out(ne + 1)

            act.wait_ge(npass_ok, 1)
            npass = act.value_load(npass_t[0:1, 0:1], min_val=1, max_val=2)
            with act.Fori(0, npass) as p:
                m0 = NE * ET * p
                with act.If(p):
                    for h in range(3):
                        split(U_MOE + h, m0)
                gathered_out(NE * p)
                gathered_high(NE * p)
                split(U_MOE + 3, m0)
                tile_silu(m0, U_MOE + 2, m0)
                split_quarters(U_MOE + 4, m0, 0, 5)
                tile_high(m0)
                step(1, m0, NE * p)
                with act.Fori(0, NE - 1) as e:
                    ne = NE * p + e
                    me = ET * ne
                    for j in range(2, ET + 2):
                        step(j, me, ne)
                ne = NE * p + (NE - 1)
                me = ET * ne
                for j in range(2, ET):
                    step(j, me, ne, more=False)
                split(U_MOE + MOE_U - 2, me)
                split(U_MOE + MOE_U - 1, me)
                y_high(ne)

            root_mean_square(4)

        @block.vector
        def _(dve):
            steps = Chain(dve, vchain)
            v = nc.vector

            def split_quarters(c, m, first, end):
                for n in range(first, end):
                    cn, cols = c + n // 2, slice(n % 2 * HALF // 2, (n % 2 + 1) * HALF // 2)
                    dve.wait_ge(hi_done, before_half(cn, m) + (n % 2 + 1))
                    v.tensor_tensor(w_lo[:, cn % RING, cols], raw[:, cn % RAW, cols],
                                    w_hi[:, cn % RING, cols].bitcast(f32), ALU.subtract).then_inc(lo_done, 1)

            def split(c, m=0):
                split_quarters(c, m, 0, 2)

            def ada_steps(u, first, end, k=0):
                a, k8 = acc[:, u % 2, :], 16 * k
                for kc in range(first, end):
                    h, cols = kc // 4, slice(kc % 4 * TW, (kc % 4 + 1) * TW)
                    if kc == 0 and u >= 2:
                        dve.wait_ge(acc_red, u - 1 + 2 * k)
                    if kc % 4 == 0:
                        dve.wait_ge(ada_in[h], 16 * (u + 1) + 32 * k)
                    if kc == 0:
                        ins = v.tensor_scalar(a, ada[:, h, cols], cond[:, 0:1], None, ALU.mult)
                    else:
                        dve.wait_ge(ada_step, 8 * u + kc + k8)
                        ins = v.scalar_tensor_tensor(a, ada[:, h, cols], cond[:, kc:kc + 1], a, ALU.mult, ALU.add)
                    ins.then_inc(ada_step, 1)

            def woven(c, m, quarters, u, chunks, k=0):
                (q0, q1), (s0, s1) = quarters, chunks
                done = s0
                for q in range(q0, q1):
                    split_quarters(c, m, q, q + 1)
                    upto = s0 + (s1 - s0) * (q - q0 + 1) // (q1 - q0)
                    ada_steps(u, done, upto, k)
                    done = upto

            def mod_out(u, bank, k=0):
                t = u if u < 3 else u + 1
                dve.wait_ge(acc_red, u + 1 + 2 * k)
                if u > 0:
                    dve.wait_ge(mod_ok, u + 2 * k)
                steps.link(v.tensor_reduce(tsum[:, :], ps[:, bank, :].rearrange("p (c q) -> p c q", c=4), AX.X, ALU.add))
                col = slice(4 * t, 4 * t + 4) if isinstance(k, int) and k == 0 else ds(8 * k + 4 * t, 4)
                v.tensor_tensor(modc[:, col], tsum[:, :], vec[:, col], ALU.add).then_inc(mod_ok, 1)

            def scale_col(q, at_scale, gain, tiles):
                dve.wait_ge(mod_ok, tiles)
                v.scalar_tensor_tensor(scol[:, q, :], modc[:, at_scale:at_scale + KC], 1.0, vec[:, gain:gain + KC],
                                       ALU.add, ALU.mult).then_inc(scol_ok, 1)

            def normed(n):
                dve.wait_ge(rs_ok, n + 1)
                steps.link(v.reciprocal(stat[:, 6:8], stat[:, 4:6]))
                for b in range(NB):
                    v.tensor_scalar((xn0 if n == 0 else xn)[:, b, :], x[:, b, :], stat[:, 6 + b:7 + b], None,
                                    ALU.mult).then_inc(xn_ok, 1)

            def modulate(q, n, shift, dst=hT_lo, hi=hT_hi):
                def bank(i):
                    dve.wait_ge(xT_done, 4 * n + i + 1)
                    if i == 1:
                        dve.wait_ge(scol_ok, q + 1)
                    if q == 3:
                        dve.wait_ge(h_ok, 4 * 2 + i + 1)
                    for c in (2 * i, 2 * i + 1):
                        ins = v.tensor_scalar(h32_at(q)[:, c, :], ps[:, i, (c % 2) * S:(c % 2 + 1) * S],
                                              scol[:, q, c:c + 1], modc[:, shift + c:shift + c + 1], ALU.mult, ALU.add)
                    ins.then_inc(h32b_ok, 1)

                def low(i):
                    dve.wait_ge(h_hi_ok, 4 * q + i + 1)
                    v.tensor_tensor(dst[:, 2 * i:2 * i + 2, :], h32_at(q)[:, 2 * i:2 * i + 2, :],
                                    hi[:, 2 * i:2 * i + 2, :].bitcast(f32), ALU.subtract).then_inc(h_ok, 1)

                bank(1)
                if dst is not None:
                    low(0)
                bank(3)
                if dst is not None:
                    low(1)
                    low(2)
                    low(3)

            def add_gated(bank, gate, tmp):
                for b in range(NB):
                    y = ps[:, bank + 2 * b:bank + 2 * b + 2, :]
                    t = tmp[:, b, :].rearrange("p (n q) -> p n q", n=2)
                    steps.link(v.tensor_tensor(t, y, gate[:, :].rearrange("p (n q) -> p n q", n=2), ALU.mult))
                    v.tensor_tensor(x[:, b, :], x[:, b, :], tmp[:, b, :], ALU.add).then_inc(x_ok, 1)

            dve.wait_ge(vecT_done, 1)
            v.tensor_copy(vec[:, :], ps[:, 4, 0:176]).then_inc(vec_ok, 1)
            dve.wait_ge(cond_ok, 1)
            ada_steps(0, 0, 8)
            dve.wait_ge(pos_in, 32)
            steps.link(v.tensor_copy(stat[:, 8:10], pos_i[:, :]))
            for b in range(NB):
                ins = v.tensor_scalar(ang[:, b, :], freq, stat[:, 8 + b:9 + b], None, ALU.mult)
            steps.link(ins)
            big = 1.5 * 2.0 ** 23
            steps.link(v.tensor_scalar(kk, ang, float(1 / (2 * np.pi)), big, ALU.mult, ALU.add))
            steps.link(v.tensor_scalar(kk, kk, big, None, ALU.subtract))
            p1 = 6.28125
            p2 = float(np.float32(np.round((2 * np.pi - p1) * 2 ** 20) / 2 ** 20))
            p3 = float(2 * np.pi - p1 - p2)
            steps.link(v.scalar_tensor_tensor(red, kk, -p1, ang, ALU.mult, ALU.add))
            steps.link(v.scalar_tensor_tensor(red, kk, -p2, red, ALU.mult, ALU.add))
            steps.link(v.scalar_tensor_tensor(red, kk, -p3, red, ALU.mult, ALU.add))
            pi = float(np.nextafter(np.float32(np.pi), np.float32(0)))
            steps.link(v.tensor_scalar(red, red, pi, -pi, ALU.min, ALU.max))
            steps.link(v.scalar_tensor_tensor(tmp_r, red, -1.0, red, ALU.mult, ALU.max))
            v.tensor_scalar(tmp_r, tmp_r, -1.0, float(np.pi / 2), ALU.mult, ALU.add).then_inc(ang_ok, 1)

            normed(0)
            ada_steps(1, 0, 8)
            mod_out(0, 6)
            ada_steps(2, 0, 8)
            mod_out(1, 7)
            dve.wait_ge(first_done, 1)
            v.tensor_tensor(modc[:, 12:16], ps[:, 5, 0:4], vec[:, 12:16], ALU.add).then_inc(first_ok, 1)
            mod_out(2, 6)
            dve.wait_ge(first_ok, 1)
            scale_col(0, MIX0 + SC, V_MIX, 3)
            split(0)
            modulate(0, 0, MIX0 + SH)
            split(1)
            split(2)

            def low_r(i):
                dve.wait_ge(outT_done, i + 1)
                for c in range(4):
                    col = V_GN + 4 * i + c
                    sc_ap = vec[:, col:col + 1] if isinstance(i, int) else vec[:, ds(4 * i + (V_GN + c), 1)]
                    ins = v.tensor_scalar(r32[:, c, :], ps[:, 6 + c // 2, (c % 2) * S:(c % 2 + 1) * S], sc_ap, None,
                                          ALU.mult)
                ins.then_inc(r32_ok, 1)
                dve.wait_ge(rTh_ok, i + 1)
                v.tensor_tensor(rT_lo[:, ds(i * 4, 4), :], r32, rT_hi[:, ds(i * 4, 4), :].bitcast(f32),
                                ALU.subtract).then_inc(rTl_ok, 1)

            def decayed(i):
                dve.wait_ge(sc_done, i + 1)
                dve.wait_ge(decay_in, 16 * i + 16)
                v.tensor_tensor(PT, ps[:, 6:8, 0:384], decay, ALU.mult).then_inc(pt_ok, 1)

            def group_norm(i):
                dve.wait_ge(pv_done, i + 1)
                for b in range(NB):
                    for hd in range(2):
                        n = 2 * b + hd
                        ins = v.bn_stats(stat[:, 40 + 6 * n:46 + 6 * n],
                                         ps[:, 4 + b, hd * DV:(hd + 1) * DV])
                steps.link(ins)
                v.memset(stat[:, 19:20], 0.0)
                for n in range(4):
                    ins = v.bn_aggr(mv[:, n, :], stat[:, 40 + 6 * n:46 + 6 * n])
                ins.then_inc(var_ok, 1)
                dve.wait_ge(var_ok, i + 1)
                dve.wait_ge(gs_ok, i + 1)
                for n in range(4):
                    b, hd = n // 2, n % 2
                    cols = slice(hd * DV, (hd + 1) * DV)
                    ins = v.scalar_tensor_tensor(gs[:, b, cols], ps[:, 4 + b, cols], mv[:, n, 0:1], gs[:, b, cols],
                                                 ALU.subtract, ALU.mult)
                steps.link(ins)
                dve.wait_ge(sd_ok, i + 1)
                steps.link(v.reciprocal(stat[:, 28:32], stat[:, 24:28]))
                for n in range(4):
                    b, hd = n // 2, n % 2
                    cols = slice(hd * DV, (hd + 1) * DV)
                    ins = v.tensor_scalar(gs[:, b, cols], gs[:, b, cols], stat[:, 28 + n:29 + n], None, ALU.mult)
                ins.then_inc(r_ok, 1)

            def pair_of_heads(i, m):
                later = not isinstance(i, int)
                if later:
                    woven(2, m, (0, 1), 3, (0, 1), m)
                    decayed(i - 1)
                    woven(2, m, (1, 4), 3, (1, 5), m)
                    group_norm(i - 1)
                    mod_out(4, 0, m - 1)
                else:
                    woven(2, m, (2, 4), 3, (0, 4), m)
                woven(2, m, (4, 6), 3, (5 if later else 4, 8), m)
                woven(2, m, (6, 8), 4, (0, 3), m)
                if later:
                    low_r(i - 1)
                woven(2, m, (8, 12), 4, (3, 8), m)
                mod_out(3, 4, m)

            pair_of_heads(0, 0)
            with dve.Fori(0, PAIRS - 1) as k:
                steps.enter(k, PAIR_STEPS)
                pair_of_heads(k + 1, k + 1)
                steps.leave(PAIRS - 1)

            woven(26, 0, (0, 1), 11, (0, 1))
            decayed(PAIRS - 1)
            woven(26, 0, (1, 3), 11, (1, 4))
            group_norm(PAIRS - 1)
            mod_out(10, 6)
            woven(26, 0, (3, 8), 11, (4, 8))
            low_r(PAIRS - 1)
            woven(26, 0, (8, 12), 12, (0, 6))
            mod_out(11, 4)
            woven(26, 0, (12, 13), 12, (6, 8))
            woven(26, 0, (13, 16), 13, (0, 4))
            mod_out(12, 5)
            split_quarters(U_FF + 2, 0, 0, 1)
            scale_col(1, FF0 + SC, V_FF, 9)
            dve.wait_ge(w_used, before_half(U_FF))
            dve.wait_ge(gbc_ev, 2)
            add_gated(0, gate_m, f_tmp)
            split_quarters(U_FF + 2, 0, 1, 2)
            ada_steps(13, 4, 5)
            normed(1)
            ada_steps(13, 5, 8)
            modulate(1, 1, FF0 + SH)

            def ff_product(j):
                if not (isinstance(j, int) and j == 0):
                    dve.wait_ge(fT_done, j)
                dve.wait_ge(fsa_ok, j + 1)
                v.tensor_tensor(f_g, ps[:, 0:2, FW:2 * FW], f_sa, ALU.mult).then_inc(fg_ok, 1)

            def ff_low(j):
                dve.wait_ge(fTh_ok, j + 1)
                v.tensor_tensor(fT_lo.rearrange("p c s -> p (c s)"), ps[:, 2, :],
                                fT_hi.rearrange("p c s -> p (c s)").bitcast(f32), ALU.subtract).then_inc(fTl_ok, 1)

            split_quarters(U_FF + 2, 0, 2, 4)
            ff_product(0)
            ff_low(0)
            split_quarters(U_FF + 2, 0, 4, 5)

            def ff_two(i):
                for o in range(2):
                    c, j = U_FF + 2 + 3 * o, 2 * i + (1 + o)
                    woven(c, i, (5, 8), 14 + o, (0, 4), i)
                    ff_product(j)
                    mod_out(13 + o, 3, i)
                    woven(c, i, (8, 11), 14 + o, (4, 6), i)
                    ff_low(j)
                    ada_steps(14 + o, 6, 8, i)

            with dve.Fori(0, 5) as k:
                steps.enter(k, 2)
                ff_two(k)
                steps.leave(5)
            split_quarters(U_KV + 1, 0, 1, 2)
            scale_col(2, KVM + SC, V_KVN, 15)
            scale_col(3, MIX1 + SC, V_MIX + KC, 19)
            split_quarters(U_KV + 1, 0, 2, 3)
            dve.wait_ge(w_used, before_half(U_KV))
            add_gated(4, gate_f, f_tmp)
            split_quarters(U_KV + 1, 0, 3, 4)
            mod_out(23, 3)

            normed(2)
            modulate(2, 2, KVM + SH)
            modulate(3, 2, MIX1 + SH, hq_lo, hq_hi)
            woven(U_KV, 0, (6, 14), 24, (0, 8))
            woven(U_KV, 0, (14, 22), 25, (0, 8))
            mod_out(24, 2)
            woven(U_KV, 0, (22, 30), 26, (0, 8))
            mod_out(25, 4)
            mod_out(26, 5)

            mask = causal[:, :].unsqueeze(1).unsqueeze(1).to_broadcast([P, 2, 2, P])

            def softplus(c):
                dve.wait_ge(sm_ok, c + 1)
                z = ps[:, 2 * (c % 3):2 * (c % 3) + 2, 0:384]
                b0, b1 = at_buf(c, 0), at_buf(c, 1)
                steps.link(v.scalar_tensor_tensor(b1, z, 0.0, b0, ALU.max, ALU.add))
                v.tensor_tensor(b0, z, b1, ALU.subtract).then_inc(z_used, 1)
                dve.wait_ge(z_used, c + 1)
                v.tensor_tensor(on_diagonal(b1), on_diagonal(b1), mask, ALU.mult).then_inc(lm_ok, 1)

            def log_weights(c):
                dve.wait_ge(tail_done, c + 1)
                v.tensor_tensor(at_buf(c, 0), at_buf(c, 0), ps[:, 2 * (c % 3):2 * (c % 3) + 2, 0:384],
                                ALU.subtract).then_inc(u_ok, 1)

            def low_o(c):
                dve.wait_ge(oh_ok, c + 1)
                v.tensor_tensor(oT_lo[:, c, :], ps[:, 6 + c % 2, 0:S], oT_hi[:, c, :].bitcast(f32),
                                ALU.subtract).then_inc(ol_ok, 1)

            for g in range(KC // 2):
                c = 2 * g
                softplus(c)
                softplus(c + 1)
                log_weights(c)
                log_weights(c + 1)
                if c:
                    low_o(c - 2)
                    low_o(c - 1)
            low_o(KC - 2)
            low_o(KC - 1)
            split_quarters(U_KV, 0, 30, 32)
            scale_col(4, FF1 + SC, V_FF + KC, 25)
            dve.wait_ge(w_used, before_half(U_MOE))
            dve.wait_ge(gbc_ev, 3)
            add_gated(0, gate_m, f_tmp)
            split_quarters(U_MOE, 0, 0, 1)
            normed(3)
            split_quarters(U_MOE, 0, 1, 2)
            modulate(4, 3, FF1 + SH, None)

            split(U_MOE + 1)
            dve.wait_ge(hk_hi_ok, 1)
            v.tensor_tensor(hk_lo.rearrange("p b (n q) -> p (b n) q", n=2), ps[:, 0:4, :],
                            hk_hi.rearrange("p b (n q) -> p (b n) q", n=2).bitcast(f32), ALU.subtract).then_inc(hk_ok, 1)
            dve.wait_ge(rt_done, 1)
            steps.link(v.tensor_copy(logit, ps[:, 4, 0:2 * NE].rearrange("p (b e) -> p b e", b=NB)))
            for b in range(NB):
                ins = v.max(mx[:, b, :], logit[:, b, :])
            steps.link(ins)
            v.tensor_tensor(stat[:, 32:34], mx[:, :, 1], mx[:, :, 0], ALU.subtract).then_inc(dm_ok, 1)
            for b in range(NB):
                ins = v.max_index(ridx[:, b, :], mx[:, b, :], logit[:, b, :])
            steps.link(ins)
            steps.link(v.tensor_copy(stat[:, 36:40].rearrange("p (b k) -> p b k", b=NB), ridx[:, :, 0:2]))
            for b in range(NB):
                for k2, oh in enumerate((oh1, oh2)):
                    ins = v.tensor_scalar(oh[:, b, :], slot_no[:, 0:NE], stat[:, 36 + 2 * b + k2:37 + 2 * b + k2], None,
                                          ALU.is_equal)
            steps.link(ins)
            v.tensor_tensor(sel, oh1, oh2, ALU.add).then_inc(sel_ok, 1)
            dve.wait_ge(ex_ok, 1)
            steps.link(v.tensor_scalar(stat[:, 10:12], stat[:, 34:36], 1.0, None, ALU.add))
            steps.link(v.reciprocal(stat[:, 12:14], stat[:, 10:12]))
            steps.link(v.tensor_tensor(stat[:, 14:16], stat[:, 12:14], stat[:, 34:36], ALU.mult))
            for b in range(NB):
                ins = v.tensor_scalar(gate_e[:, b, :], oh1[:, b, :], stat[:, 12 + b:13 + b], None, ALU.mult)
            steps.link(ins)
            for b in range(NB):
                ins = v.scalar_tensor_tensor(gate_e[:, b, :], oh2[:, b, :], stat[:, 14 + b:15 + b], gate_e[:, b, :],
                                             ALU.mult, ALU.add)
            steps.link(ins)
            dve.wait_ge(cnt_done, 1)
            def one_hot(ne, e):
                for b in range(NB):
                    ins = v.tensor_scalar(hot[:, b, :], slot_no[:, :], slot[:, b, ds(e, 1)], sel[:, b, ds(e, 1)],
                                          ALU.is_equal, ALU.mult)
                ins.then_inc(hot_ok, 1)

            steps.link(v.tensor_copy(slot, ps[:, 5, 0:2 * NE].rearrange("p (b e) -> p b e", b=NB)))
            one_hot(0, 0)
            steps.link(v.tensor_reduce(stat[:, 16:17], ps[:, 5, 2 * NE:3 * NE], AX.X, ALU.max))
            v.tensor_scalar(npass_t[:, :], stat[:, 16:17], float(P), 1.0, ALU.is_gt, ALU.add).then_inc(npass_ok, 1)

            split(U_MOE + 2)

            def tile_product(n, c, m):
                dve.wait_ge(esa_ok, n + 1)
                dve.wait_ge(w_used, before_half(c, m))
                v.tensor_tensor(e_g, ps[:, 1, :], e_sa, ALU.mult).then_inc(eg_ok, 1)

            def tile_low(n):
                dve.wait_ge(eTh_ok, n + 1)
                v.tensor_tensor(eT_lo.rearrange("p c s -> p (c s)"), ps[:, 2, :],
                                eT_hi.rearrange("p c s -> p (c s)").bitcast(f32), ALU.subtract).then_inc(eTl_ok, 1)

            def gathered_low(ne):
                dve.wait_ge(hgh_ok, ne + 1)
                v.tensor_tensor(hg_lo.rearrange("p (n c) s -> p n (c s)", n=2), ps[:, 6:8, :],
                                hg_hi.rearrange("p (n c) s -> p n (c s)", n=2).bitcast(f32),
                                ALU.subtract).then_inc(hgl_ok, 1)

            def y_gated(ne, c, m):
                dve.wait_ge(w_used, before_half(c, m))
                v.tensor_tensor(y32.rearrange("p (n q) -> p n q", n=2), ps[:, 4:6, :],
                                gate_f[:, :].rearrange("p (n q) -> p n q", n=2), ALU.mult).then_inc(yg_ok, 1)

            def y_low(ne):
                dve.wait_ge(yh_ok, ne + 1)
                v.tensor_tensor(y_lo, y32, y_hi.bitcast(f32), ALU.subtract).then_inc(yl_ok, 1)

            def accumulate(ne, e):
                for b in range(NB):
                    dve.wait_ge(scat_done, NB * ne + b + 1)
                    xb = x[:, b, :].rearrange("p (n q) -> p n q", n=2)
                    v.scalar_tensor_tensor(xb, ps[:, 6 - 2 * b:8 - 2 * b, :], gate_e[:, b, ds(e, 1)], xb,
                                           ALU.mult, ALU.add).then_inc(yacc_ok, 1)

            def step(j, me, ne, e, more=True):
                c, n = U_MOE + 4 + RAW * (j - 1), me + j
                split_quarters(c, me, 5, 9)
                if j == ET + 1:
                    accumulate(ne, e)
                split_quarters(c, me, 9, 12)
                if j < ET - 1 or more:
                    split_quarters(c, me, 12, 13)
                dve.wait_ge(eT_done, n)
                tile_product(n, c + 4, me)
                if j < ET - 1 or more:
                    split_quarters(c, me, 13, 14)
                    if j == ET - 1:
                        gathered_low(ne + 1)
                    split_quarters(c, me, 14, 17)
                if j == ET:
                    y_gated(ne, c + 6, me)
                tile_low(n)
                if j == ET:
                    y_low(ne)
                if j == ET - 3 and more:
                    dve.wait_ge(hotT_done, ne + 1)
                    one_hot(ne + 1, e + 1)

            dve.wait_ge(npass_ok, 1)
            npass = dve.value_load(npass_t[0:1, 0:1], min_val=1, max_val=2)
            dve.wait_ge(gbc_ev, 4)
            with dve.Fori(0, npass) as p:
                steps.enter(p, 1)
                m0 = NE * ET * p
                with dve.If(p):
                    for h in range(3):
                        split(U_MOE + h, m0)
                    one_hot(NE * p, 0)
                gathered_low(NE * p)
                split(U_MOE + 3, m0)
                split_quarters(U_MOE + 4, m0, 0, 1)
                tile_product(m0, U_MOE + 4, m0)
                split_quarters(U_MOE + 4, m0, 1, 5)
                tile_low(m0)
                step(1, m0, NE * p, 0)
                with dve.Fori(0, NE - 1) as e:
                    ne = NE * p + e
                    me = ET * ne
                    for j in range(2, ET + 2):
                        step(j, me, ne, e)
                ne = NE * p + (NE - 1)
                me = ET * ne
                for j in range(2, ET):
                    step(j, me, ne, NE - 1, more=False)
                split(U_MOE + MOE_U - 2, me)
                split(U_MOE + MOE_U - 1, me)
                y_gated(ne, U_MOE + MOE_U, me)
                y_low(ne)
                accumulate(ne, NE - 1)
                steps.link(v.tensor_scalar(slot, slot, -float(P), None, ALU.add))
                steps.leave(npass)

            dve.wait_ge(fnorm_in, 16)
            dve.wait_ge(rs_ok, 5)
            steps.link(v.reciprocal(stat[:, 6:8], stat[:, 4:6]))
            for b in range(NB):
                v.scalar_tensor_tensor(x[:, b, :], x[:, b, :], stat[:, 6 + b:7 + b], fnorm, ALU.mult,
                                       ALU.mult).then_inc(o_ok, 1)


class Chain:

    def __init__(self, engine, semaphore):
        self.engine, self.semaphore, self.n, self.base, self.kept = engine, semaphore, 0, 0, []

    def link(self, instruction):
        self.n += 1
        instruction.then_inc(self.semaphore, 1)
        self.engine.wait_ge(self.semaphore, self.base + self.n)

    def enter(self, register, per_turn):
        self.kept.append((self.base, self.n, per_turn))
        self.base = self.base + register * per_turn

    def leave(self, turns):
        base, n, per_turn = self.kept.pop()
        assert self.n - n == per_turn, (self.n - n, per_turn)
        self.base, self.n = (base, n + turns * per_turn) if isinstance(turns, int) else (base + turns * per_turn, n)


_INS = ["x", "c", "positions", "ada_w", "ada_b", "norm_mix", "norm_ff", "ret_w_in", "ret_gn", "ret_w_out",
        "kv_ada_w", "kv_ada_b", "kv_norm", "kv_w", "sb_w_q", "sb_w_out", "ff_w_in", "ff_w_out", "moe_router",
        "moe_w_in", "moe_w_out", "final_norm"]


def _constants():
    log_gamma = np.log(1.0 - np.exp2(-5.0 - np.arange(RET_HEADS)))
    m, n = np.arange(S)[:, None], np.arange(S)[None, :]
    table = np.exp(np.abs(m - n)[None] * log_gamma[:, None, None]) * (m // CHUNK <= n // CHUNK) * DK ** -0.5
    both = np.concatenate([table[:, :P, :], table[:, P:, P:]], axis=2)
    decay = both.reshape(PAIRS, 2, P, 384).transpose(0, 2, 1, 3).reshape(PAIRS * P, 768)
    freq = 10000.0 ** (-np.arange(0, DK, 2) / DK)
    return decay.astype(np.float32), freq.astype(np.float32)[None, :]


def kernel(**inputs):
    import concourse.bacc as bacc
    from concourse.bass_utils import run_bass_kernel_spmd

    nc = bacc.Bacc("TRN2", target_bir_lowering=False, num_devices=1, dynamic_dma_scratch_size=DMA_SCRATCH)
    decay, freq = _constants()
    given = {name: inputs[name] for name in _INS} | {"decay_table": decay, "frequencies": freq}
    arrays, args = {}, []
    for name, value in given.items():
        a = np.ascontiguousarray(value)
        arrays[f"in_{name}"] = a
        args.append(nc.dram_tensor(f"in_{name}", a.shape, mybir.dt.from_np(a.dtype), kind="ExternalInput").ap())
    out = nc.dram_tensor("out_x", (1, S, D), mybir.dt.float32, kind="ExternalOutput").ap()
    trunk(nc, *args, out)
    r = run_bass_kernel_spmd(nc, [arrays], core_ids=[0])
    return r.results[0]["out_x"]
```
